# Optimizing a Trainium2 kernel written in Bass

```python
import math
import jax, jax.numpy as jnp
from jax import lax
import numpy as np

D_MODEL = 1024
BATCH = 1
SEQ = 512
DEPTH = 1

HEAD_DIM = 64
BLK = 128
A_GROUPS = ((128, 1), (512, 4), (2048, 16))
A_HEADS = 4
B_Q_HEADS = 8
B_KV_HEADS = 2
B_WINDOW = 128
C_HEADS = 4
N_BRANCH = 3
NUM_BUCKETS = 32
MAX_DISTANCE = max(w for w, _ in A_GROUPS)
D_FF = 4 * D_MODEL
CONV_WIDTH = 3
EPS = 1e-6

A_WIDTH = A_HEADS * HEAD_DIM
B_WIDTH = B_Q_HEADS * HEAD_DIM
C_WIDTH = C_HEADS * HEAD_DIM
B_GROUP = B_Q_HEADS // B_KV_HEADS
N_A_GROUP_HEADS = len(A_GROUPS) * A_HEADS
N_BIAS_HEADS = N_A_GROUP_HEADS + B_Q_HEADS
A_QKV_COLS = 3 * N_A_GROUP_HEADS * HEAD_DIM
B_Q_COLS = B_WIDTH
B_KV_COLS = 2 * B_KV_HEADS * HEAD_DIM
C_QKV_COLS = 3 * C_WIDTH
GATE_COLS = N_BRANCH * D_MODEL
OFF_B_Q = A_QKV_COLS
OFF_B_KV = OFF_B_Q + B_Q_COLS
OFF_C = OFF_B_KV + B_KV_COLS
OFF_GATE = OFF_C + C_QKV_COLS
IN_COLS = OFF_GATE + GATE_COLS
SCALE = HEAD_DIM ** -0.5


def rms_norm(x, g):
    xf = x.astype(jnp.float32)
    y = xf * lax.rsqrt(jnp.mean(xf * xf, axis=-1, keepdims=True) + EPS)
    return (y * g.astype(jnp.float32)).astype(x.dtype)

def t5_bucket(dist):
    max_exact = NUM_BUCKETS // 2
    nf = jnp.maximum(dist, 1).astype(jnp.float32)
    large = max_exact + (jnp.log(nf / max_exact) / math.log(MAX_DISTANCE / max_exact)
                         * (NUM_BUCKETS - max_exact)).astype(jnp.int32)
    large = jnp.minimum(large, NUM_BUCKETS - 1)
    return jnp.where(dist < max_exact, dist, large)

def band_layout(n_blocks, max_dist):
    a = jnp.arange(BLK)[:, None]
    b = jnp.arange(2 * BLK)[None, :]
    dist = a + BLK - b
    in_band = (dist >= 0) & (dist <= max_dist)
    key_exists = (jnp.arange(n_blocks)[:, None] > 0) | (jnp.arange(2 * BLK)[None, :] >= BLK)
    mask = in_band[None] & key_exists[:, None, :]
    return jnp.maximum(dist, 0), mask

def band_bias(table, dist):
    return jnp.transpose(table[t5_bucket(dist)], (2, 0, 1)).astype(jnp.float32)

def banded_attention(q, k, v, bias, mask):
    n, hkv, g, L, dh = q.shape
    nb = L // BLK
    qb = q.reshape(n, hkv, g, nb, BLK, dh)

    def two_blocks(t):
        tb = t.reshape(n, hkv, nb, BLK, dh)
        prev = jnp.pad(tb, ((0, 0), (0, 0), (1, 0), (0, 0), (0, 0)))[:, :, :nb]
        return jnp.concatenate([prev, tb], axis=3)

    kw, vw = two_blocks(k), two_blocks(v)
    logits = jnp.einsum('nkgbqd,nkbsd->nkgbqs', qb, kw, preferred_element_type=jnp.float32) * SCALE
    logits = jnp.where(mask, logits + bias[:, :, None], -jnp.inf)
    m = jnp.max(logits, axis=-1)
    p = jnp.exp(logits - m[..., None])
    l = jnp.sum(p, axis=-1)
    num = jnp.einsum('nkgbqs,nkbsd->nkgbqd', p, vw.astype(jnp.float32))
    return num.reshape(n, hkv, g, L, dh), m.reshape(n, hkv, g, L), l.reshape(n, hkv, g, L)

def to_sub(t, d, lp):
    b, s, h, dh = t.shape
    L = s // d
    t = t.reshape(b, L, d, h, dh).transpose(0, 2, 3, 1, 4).reshape(b * d, h, L, dh)
    return jnp.pad(t, ((0, 0), (0, 0), (0, lp - L), (0, 0)))

def dilated_attention(q, k, v, table_a):
    b, s = q.shape[:2]
    nums, ms, ls = [], [], []
    for gi, (window, d) in enumerate(A_GROUPS):
        L = s // d
        lp = -(-L // BLK) * BLK
        dist, mask = band_layout(lp // BLK, window // d)
        bias = band_bias(table_a[:, gi], dist * d)[:, None]
        num, m, l = banded_attention(to_sub(q[:, :, gi], d, lp)[:, :, None],
                                     to_sub(k[:, :, gi], d, lp), to_sub(v[:, :, gi], d, lp), bias, mask)
        num = num[:, :, 0, :L].reshape(b, d, A_HEADS, L, HEAD_DIM).transpose(0, 3, 1, 2, 4)
        nums.append(num.reshape(b, s, A_HEADS, HEAD_DIM))
        ms.append(m[:, :, 0, :L].reshape(b, d, A_HEADS, L).transpose(0, 3, 1, 2).reshape(b, s, A_HEADS))
        ls.append(l[:, :, 0, :L].reshape(b, d, A_HEADS, L).transpose(0, 3, 1, 2).reshape(b, s, A_HEADS))
    nums = jnp.stack(nums, axis=2)
    ms = jnp.stack(ms, axis=2)
    ls = jnp.stack(ls, axis=2)
    c = jnp.exp(ms - jnp.max(ms, axis=2, keepdims=True))
    out = jnp.sum(c[..., None] * nums, axis=2) / jnp.sum(c * ls, axis=2)[..., None]
    return out.reshape(b, s, A_WIDTH).astype(q.dtype)

def sliding_window_gqa(q, k, v, sinks, table_b):
    b, s = q.shape[:2]
    dist, mask = band_layout(s // BLK, B_WINDOW - 1)
    bias = band_bias(table_b, dist).reshape(B_KV_HEADS, B_GROUP, BLK, 2 * BLK)
    qh = q.reshape(b, s, B_KV_HEADS, B_GROUP, HEAD_DIM).transpose(0, 2, 3, 1, 4)
    num, m, l = banded_attention(qh, k.transpose(0, 2, 1, 3), v.transpose(0, 2, 1, 3), bias, mask)
    sink = sinks.reshape(B_KV_HEADS, B_GROUP)[None, :, :, None].astype(jnp.float32)
    mx = jnp.maximum(m, sink)
    c = jnp.exp(m - mx)
    out = num * (c / (l * c + jnp.exp(sink - mx)))[..., None]
    return out.transpose(0, 3, 1, 2, 4).reshape(b, s, B_WIDTH).astype(q.dtype)

def stick_breaking_attention(q, k, v):
    b, s = q.shape[:2]
    qh, kh, vh = (t.transpose(0, 2, 1, 3) for t in (q, k, v))
    outs = []
    for i in range(s // BLK):
        lo, hi = i * BLK, (i + 1) * BLK
        z = jnp.einsum('bhqd,bhsd->bhqs', qh[:, :, lo:hi], kh[:, :, :hi],
                       preferred_element_type=jnp.float32) * SCALE
        before = jnp.arange(hi)[None, :] < jnp.arange(lo, hi)[:, None]
        log_keep = jnp.where(before, jax.nn.log_sigmoid(-z), 0.0)
        log_rest = lax.cumsum(log_keep, axis=3, reverse=True) - log_keep
        wts = jnp.where(before, jnp.exp(jax.nn.log_sigmoid(z) + log_rest), 0.0)
        outs.append(jnp.einsum('bhqs,bhsd->bhqd', wts, vh[:, :, :hi].astype(jnp.float32)))
    out = jnp.concatenate(outs, axis=2).transpose(0, 2, 1, 3)
    return out.reshape(b, s, C_WIDTH).astype(q.dtype)

def hybrid_mixer(h, rel_bias, w_in, b_gate, sinks, w_br_a, w_br_b, w_br_c, w_out):
    b, s, _ = h.shape
    proj = h @ w_in
    a_qkv, b_q, b_kv, c_qkv, gates = jnp.split(proj, [OFF_B_Q, OFF_B_KV, OFF_C, OFF_GATE], axis=-1)
    a_qkv = a_qkv.reshape(b, s, 3, len(A_GROUPS), A_HEADS, HEAD_DIM)
    table_a = rel_bias[:, :N_A_GROUP_HEADS].reshape(NUM_BUCKETS, len(A_GROUPS), A_HEADS)
    o_a = dilated_attention(a_qkv[:, :, 0], a_qkv[:, :, 1], a_qkv[:, :, 2], table_a)
    b_kv = b_kv.reshape(b, s, 2, B_KV_HEADS, HEAD_DIM)
    o_b = sliding_window_gqa(b_q.reshape(b, s, B_Q_HEADS, HEAD_DIM), b_kv[:, :, 0], b_kv[:, :, 1],
                             sinks, rel_bias[:, N_A_GROUP_HEADS:])
    c_qkv = c_qkv.reshape(b, s, 3, C_HEADS, HEAD_DIM)
    o_c = stick_breaking_attention(c_qkv[:, :, 0], c_qkv[:, :, 1], c_qkv[:, :, 2])
    g = jax.nn.sigmoid(gates.reshape(b, s, N_BRANCH, D_MODEL) + b_gate)
    merged = g[:, :, 0] * (o_a @ w_br_a) + g[:, :, 1] * (o_b @ w_br_b) + g[:, :, 2] * (o_c @ w_br_c)
    return merged @ w_out

def conv_ffn(h, w_up, conv_w, conv_b, w_down):
    u = h @ w_up
    u = lax.conv_general_dilated(u, conv_w[:, None, :], window_strides=(1,),
                                 padding=[(CONV_WIDTH - 1, 0)],
                                 dimension_numbers=('NWC', 'WIO', 'NWC'),
                                 feature_group_count=u.shape[-1]) + conv_b
    gate, val = jnp.split(u, 2, axis=-1)
    return (jax.nn.gelu(gate, approximate=True) * val) @ w_down

def first_inputs(seed: int = 0) -> dict:
    key = jax.random.key(seed)
    ks = jax.random.split(key, 17)

    def nrm(k, shape, scale):
        return jax.random.normal(k, shape, jnp.float32) * scale

    def gain(k):
        return 1.0 + nrm(k, (DEPTH, D_MODEL), 0.1)

    return {
        'x': nrm(ks[0], (BATCH, SEQ, D_MODEL), 1.0),
        'rel_bias': nrm(ks[1], (NUM_BUCKETS, N_BIAS_HEADS), 0.5),
        'attn_pre_norm': gain(ks[2]),
        'w_in': nrm(ks[3], (DEPTH, D_MODEL, IN_COLS), D_MODEL ** -0.5),
        'b_gate': nrm(ks[4], (DEPTH, N_BRANCH, D_MODEL), 0.1),
        'sinks': nrm(ks[5], (DEPTH, B_Q_HEADS), 0.5),
        'w_br_a': nrm(ks[6], (DEPTH, A_WIDTH, D_MODEL), A_WIDTH ** -0.5),
        'w_br_b': nrm(ks[7], (DEPTH, B_WIDTH, D_MODEL), B_WIDTH ** -0.5),
        'w_br_c': nrm(ks[8], (DEPTH, C_WIDTH, D_MODEL), C_WIDTH ** -0.5),
        'w_out': nrm(ks[9], (DEPTH, D_MODEL, D_MODEL), D_MODEL ** -0.5),
        'attn_post_norm': gain(ks[10]),
        'ffn_pre_norm': gain(ks[11]),
        'w_up': nrm(ks[12], (DEPTH, D_MODEL, 2 * D_FF), D_MODEL ** -0.5),
        'conv_w': nrm(ks[13], (DEPTH, CONV_WIDTH, 2 * D_FF), CONV_WIDTH ** -0.5),
        'conv_b': nrm(ks[14], (DEPTH, 2 * D_FF), 0.02),
        'w_down': nrm(ks[15], (DEPTH, D_FF, D_MODEL), D_FF ** -0.5),
        'ffn_post_norm': gain(ks[16]),
    }

def first_block(x, rel_bias, attn_pre_norm, w_in, b_gate, sinks, w_br_a, w_br_b, w_br_c, w_out,
              attn_post_norm, ffn_pre_norm, w_up, conv_w, conv_b, w_down, ffn_post_norm):
    for layer in range(DEPTH):
        h = rms_norm(x, attn_pre_norm[layer])
        h = hybrid_mixer(h, rel_bias, w_in[layer], b_gate[layer], sinks[layer],
                         w_br_a[layer], w_br_b[layer], w_br_c[layer], w_out[layer])
        x = x + rms_norm(h, attn_post_norm[layer])
        h = rms_norm(x, ffn_pre_norm[layer])
        h = conv_ffn(h, w_up[layer], conv_w[layer], conv_b[layer], w_down[layer])
        x = x + rms_norm(h, ffn_post_norm[layer])
    return x


DEPTH_2 = 2

N_META = 16
CHUNK = 128
D_MIX = D_MODEL
RET_HEADS = 4
RET_DK = 128
RET_DV = 128
RET_WIDTH = RET_HEADS * RET_DV
RET_THETA = 10000.0
DIFF_HEADS = 4
DIFF_D = 64
DIFF_DV = 2 * DIFF_D
DIFF_WIDTH = DIFF_HEADS * DIFF_DV
ROPE_THETA = 500000.0
ROPE_DIMS = DIFF_D // 4
D_FF_2 = 2816

IN_SIZES = (
    RET_HEADS * RET_DK,
    RET_HEADS * RET_DK,
    RET_WIDTH,
    RET_WIDTH,
    DIFF_HEADS * 2 * DIFF_D,
    DIFF_HEADS * 2 * DIFF_D,
    DIFF_WIDTH,
)
D_IN = sum(IN_SIZES)


def rmsnorm(x, g):
    xf = x.astype(jnp.float32)
    y = xf * lax.rsqrt(jnp.mean(xf * xf, axis=-1, keepdims=True) + EPS)
    return (y * g.astype(jnp.float32)).astype(x.dtype)

def swiglu(x, w_gate, w_up, w_down):
    return (jax.nn.silu(x @ w_gate) * (x @ w_up)) @ w_down

def retention_rotate(x, pos):
    d = x.shape[-1]
    angle = RET_THETA ** (-jnp.linspace(0.0, 1.0, d // 2, dtype=jnp.float32))
    freqs = pos[:, None] * angle[None, :]
    cos = jnp.cos(freqs)[None, :, None, :]
    sin = jnp.sin(freqs)[None, :, None, :]
    x1, x2 = x[..., 0::2], x[..., 1::2]
    out = jnp.stack([x1 * cos - x2 * sin, x1 * sin + x2 * cos], axis=-1)
    return out.reshape(x.shape)

def partial_rope(x, pos):
    r = ROPE_DIMS
    inv = ROPE_THETA ** (-jnp.arange(0, r, 2, dtype=jnp.float32) / r)
    freqs = pos[:, None] * inv[None, :]
    emb = jnp.concatenate([freqs, freqs], axis=-1)
    cos = jnp.cos(emb)[None, :, None, None, :]
    sin = jnp.sin(emb)[None, :, None, None, :]
    xr, xp = x[..., :r], x[..., r:]
    rot = jnp.concatenate([-xr[..., r // 2:], xr[..., :r // 2]], axis=-1)
    return jnp.concatenate([xr * cos + rot * sin, xp], axis=-1)

def retention_group(q, k, v, g, gn_w):
    B, T = q.shape[0], q.shape[1]
    f32 = jnp.float32
    pos = jnp.arange(T, dtype=f32)
    q = retention_rotate(q.reshape(B, T, RET_HEADS, RET_DK).astype(f32), pos)
    k = retention_rotate(k.reshape(B, T, RET_HEADS, RET_DK).astype(f32), pos) * (RET_DK ** -0.5)
    v = v.reshape(B, T, RET_HEADS, RET_DV).astype(f32)

    n_chunks = -(-T // CHUNK)
    pad = n_chunks * CHUNK - T

    def to_chunks(t):
        t = jnp.pad(t, ((0, 0), (pad, 0), (0, 0), (0, 0)))
        return t.reshape(B, n_chunks, CHUNK, t.shape[2], t.shape[3]).transpose(0, 3, 1, 2, 4)

    qc, kc, vc = to_chunks(q), to_chunks(k), to_chunks(v)

    log_gamma = jnp.log(1.0 - 2.0 ** (-5.0 - jnp.arange(RET_HEADS, dtype=f32)))
    idx = jnp.arange(CHUNK, dtype=f32)
    rel = idx[:, None] - idx[None, :]
    decay_intra = jnp.where(rel >= 0, jnp.exp(log_gamma[:, None, None] * jnp.maximum(rel, 0.0)), 0.0)
    k_decay = jnp.exp(log_gamma[:, None] * (CHUNK - 1 - idx)[None, :])
    q_decay = jnp.exp(log_gamma[:, None] * (idx + 1.0)[None, :])
    chunk_decay = jnp.exp(log_gamma * CHUNK)

    scores = jnp.einsum('bhnid,bhnjd->bhnij', qc, kc) * decay_intra[None, :, None]
    o_intra = jnp.einsum('bhnij,bhnje->bhnie', scores, vc)

    chunk_state = jnp.einsum('bhnjd,bhnje,hj->bhnde', kc, vc, k_decay)

    def step(R, s):
        return R * chunk_decay[None, :, None, None] + s, R

    R0 = jnp.zeros((B, RET_HEADS, RET_DK, RET_DV), f32)
    _, R_prev = lax.scan(step, R0, jnp.moveaxis(chunk_state, 2, 0))
    R_prev = jnp.moveaxis(R_prev, 0, 2)
    o_cross = jnp.einsum('bhnid,bhnde,hi->bhnie', qc, R_prev, q_decay)

    o = (o_intra + o_cross).transpose(0, 2, 3, 1, 4).reshape(B, n_chunks * CHUNK, RET_HEADS, RET_DV)[:, pad:]
    mu = jnp.mean(o, axis=-1, keepdims=True)
    var = jnp.mean((o - mu) ** 2, axis=-1, keepdims=True)
    o = ((o - mu) * lax.rsqrt(var + EPS)).reshape(B, T, RET_WIDTH) * gn_w.astype(f32)
    return (jax.nn.silu(g.astype(f32)) * o).astype(g.dtype)

def diff_attention_group(q, k, v, subln_w, lq1, lk1, lq2, lk2, lambda_init):
    B, T = q.shape[0], q.shape[1]
    f32 = jnp.float32
    pos = jnp.arange(T, dtype=f32)
    q = partial_rope(q.reshape(B, T, DIFF_HEADS, 2, DIFF_D).astype(f32), pos)
    k = partial_rope(k.reshape(B, T, DIFF_HEADS, 2, DIFF_D).astype(f32), pos)
    v = v.reshape(B, T, DIFF_HEADS, DIFF_DV).astype(f32)

    lam = (jnp.exp(jnp.sum(lq1.astype(f32) * lk1.astype(f32)))
           - jnp.exp(jnp.sum(lq2.astype(f32) * lk2.astype(f32))) + lambda_init)

    n_blocks = -(-T // CHUNK)
    pad = n_blocks * CHUNK - T
    q = jnp.pad(q, ((0, 0), (pad, 0), (0, 0), (0, 0), (0, 0))).transpose(0, 2, 3, 1, 4)
    k = jnp.pad(k, ((0, 0), (pad, 0), (0, 0), (0, 0), (0, 0))).transpose(0, 2, 3, 1, 4)
    v = jnp.pad(v, ((0, 0), (pad, 0), (0, 0), (0, 0))).transpose(0, 2, 1, 3)
    scale = DIFF_D ** -0.5

    outs = []
    for nb in range(n_blocks):
        n_keys = (nb + 1) * CHUNK
        qb = q[:, :, :, nb * CHUNK:(nb + 1) * CHUNK]
        s = jnp.einsum('bhmid,bhmjd->bhmij', qb, k[:, :, :, :n_keys]) * scale
        qi = nb * CHUNK + jnp.arange(CHUNK)
        kj = jnp.arange(n_keys)
        allowed = (kj[None, :] <= qi[:, None]) & (kj[None, :] >= pad)
        p = jax.nn.softmax(jnp.where(allowed, s, -1e30), axis=-1)
        a = p[:, :, 0] - lam * p[:, :, 1]
        outs.append(jnp.einsum('bhij,bhje->bhie', a, v[:, :, :n_keys]))
    o = jnp.concatenate(outs, axis=2)[:, :, pad:].transpose(0, 2, 1, 3)
    o = o * lax.rsqrt(jnp.mean(o * o, axis=-1, keepdims=True) + EPS) * subln_w.astype(f32)
    o = o * (1.0 - lambda_init)
    return o.reshape(B, T, DIFF_WIDTH).astype(q.dtype)

def second_inputs(seed: int = 0) -> dict:
    key = jax.random.key(seed)
    ks = jax.random.split(key, 24)
    f32 = jnp.float32
    nrm = lambda k, shape, s: jax.random.normal(k, shape, f32) * s
    gain = lambda k, shape: 1.0 + 0.1 * jax.random.normal(k, shape, f32)
    return {
        "x": jax.random.normal(ks[0], (BATCH, SEQ, D_MODEL), f32),
        "meta_tokens": nrm(ks[1], (N_META, D_MODEL), 1.0),
        "ffn1_norm": gain(ks[2], (DEPTH_2, D_MODEL)),
        "ffn1_w_gate": nrm(ks[3], (DEPTH_2, D_MODEL, D_FF_2), D_MODEL ** -0.5),
        "ffn1_w_up": nrm(ks[4], (DEPTH_2, D_MODEL, D_FF_2), D_MODEL ** -0.5),
        "ffn1_w_down": nrm(ks[5], (DEPTH_2, D_FF_2, D_MODEL), D_FF_2 ** -0.5),
        "mix_norm": gain(ks[6], (DEPTH_2, D_MODEL)),
        "w_in": nrm(ks[7], (DEPTH_2, D_MODEL, D_IN), D_MODEL ** -0.5),
        "ret_gn_w": gain(ks[8], (DEPTH_2, RET_WIDTH)),
        "diff_subln_w": gain(ks[9], (DEPTH_2, DIFF_DV)),
        "diff_lambda_q1": nrm(ks[10], (DEPTH_2, DIFF_D), 0.1),
        "diff_lambda_k1": nrm(ks[11], (DEPTH_2, DIFF_D), 0.1),
        "diff_lambda_q2": nrm(ks[12], (DEPTH_2, DIFF_D), 0.1),
        "diff_lambda_k2": nrm(ks[13], (DEPTH_2, DIFF_D), 0.1),
        "w_out": nrm(ks[14], (DEPTH_2, D_MIX, D_MODEL), D_MIX ** -0.5),
        "ffn2_norm": gain(ks[15], (DEPTH_2, D_MODEL)),
        "ffn2_w_gate": nrm(ks[16], (DEPTH_2, D_MODEL, D_FF_2), D_MODEL ** -0.5),
        "ffn2_w_up": nrm(ks[17], (DEPTH_2, D_MODEL, D_FF_2), D_MODEL ** -0.5),
        "ffn2_w_down": nrm(ks[18], (DEPTH_2, D_FF_2, D_MODEL), D_FF_2 ** -0.5),
        "final_norm": gain(ks[19], (D_MODEL,)),
    }

def second_block(x, meta_tokens, ffn1_norm, ffn1_w_gate, ffn1_w_up, ffn1_w_down,
              mix_norm, w_in, ret_gn_w, diff_subln_w, diff_lambda_q1, diff_lambda_k1,
              diff_lambda_q2, diff_lambda_k2, w_out, ffn2_norm, ffn2_w_gate,
              ffn2_w_up, ffn2_w_down, final_norm):
    B = x.shape[0]
    meta = jnp.broadcast_to(meta_tokens.astype(x.dtype)[None], (B, N_META, D_MODEL))
    h = jnp.concatenate([meta, x], axis=1)
    offs = np.cumsum((0,) + IN_SIZES)

    for l in range(DEPTH_2):
        h = h + 0.5 * swiglu(rmsnorm(h, ffn1_norm[l]), ffn1_w_gate[l], ffn1_w_up[l], ffn1_w_down[l])

        proj = rmsnorm(h, mix_norm[l]) @ w_in[l]
        parts = [proj[..., int(offs[i]):int(offs[i + 1])] for i in range(len(IN_SIZES))]
        rq, rk, rv, rg, dq, dk, dv = parts
        lambda_init = 0.8 - 0.6 * math.exp(-0.3 * l)
        y_ret = retention_group(rq, rk, rv, rg, ret_gn_w[l])
        y_diff = diff_attention_group(dq, dk, dv, diff_subln_w[l], diff_lambda_q1[l],
                                      diff_lambda_k1[l], diff_lambda_q2[l], diff_lambda_k2[l],
                                      lambda_init)
        h = h + jnp.concatenate([y_ret, y_diff], axis=-1) @ w_out[l]

        h = h + 0.5 * swiglu(rmsnorm(h, ffn2_norm[l]), ffn2_w_gate[l], ffn2_w_up[l], ffn2_w_down[l])

    h = rmsnorm(h, final_norm)
    return h[:, N_META:]


def setup_inputs(seed=0):
    out = dict(first_inputs(seed))
    for name, value in second_inputs(seed + 1).items():
        if name != "x":
            out[name + "_2"] = value
    return out


def reference(
    x, rel_bias, attn_pre_norm, w_in, b_gate, sinks, w_br_a, w_br_b, w_br_c, w_out,
    attn_post_norm, ffn_pre_norm, w_up, conv_w, conv_b, w_down, ffn_post_norm, meta_tokens_2,
    ffn1_norm_2, ffn1_w_gate_2, ffn1_w_up_2, ffn1_w_down_2, mix_norm_2, w_in_2, ret_gn_w_2,
    diff_subln_w_2, diff_lambda_q1_2, diff_lambda_k1_2, diff_lambda_q2_2, diff_lambda_k2_2,
    w_out_2, ffn2_norm_2, ffn2_w_gate_2, ffn2_w_up_2, ffn2_w_down_2, final_norm_2,
):
    x = first_block(
        x, rel_bias, attn_pre_norm, w_in, b_gate, sinks, w_br_a, w_br_b, w_br_c, w_out,
        attn_post_norm, ffn_pre_norm, w_up, conv_w, conv_b, w_down, ffn_post_norm,
    )
    return second_block(
        x, meta_tokens_2, ffn1_norm_2, ffn1_w_gate_2, ffn1_w_up_2, ffn1_w_down_2, mix_norm_2,
        w_in_2, ret_gn_w_2, diff_subln_w_2, diff_lambda_q1_2, diff_lambda_k1_2,
        diff_lambda_q2_2, diff_lambda_k2_2, w_out_2, ffn2_norm_2, ffn2_w_gate_2, ffn2_w_up_2,
        ffn2_w_down_2, final_norm_2,
    )


_drawn_inputs = setup_inputs


def setup_inputs(seed=0):
    import zlib

    import numpy as np

    out = dict(_drawn_inputs(seed))
    spreads = {}
    factors = {'sinks': 4.407, 'diff_lambda_k1_2': 6.89, 'diff_lambda_k2_2': 8.0}
    for name, (base, spread) in spreads.items():
        noise = np.random.default_rng([zlib.crc32(name.encode()), seed]).standard_normal(out[name].shape)
        drawn = base * np.exp(spread * noise) if base else spread * noise
        out[name] = __import__('jax').numpy.asarray(drawn.astype(out[name].dtype))
    for name, factor in factors.items():
        out[name] = (out[name] * factor).astype(out[name].dtype)
    return out
```

```python
import math
from contextlib import ExitStack

import numpy as np
import concourse.bass as bass
from concourse import mybir

F32 = mybir.dt.float32
F32R = mybir.dt.float32r
ACT = mybir.ActivationFunctionType
ALU = mybir.AluOpType
AX = mybir.AxisListType

P = 128
DM = 1024
KT = DM // P
SEQ = 512
META = 16
T1, T2 = SEQ, SEQ + META
NBLK = SEQ // P
EPS = 1e-6
NEG = -1e30
HD = 64
SCALE = HD ** -0.5

A_HEADS, B_HEADS, C_HEADS = 4, 8, 4
FF1_TILES = 4096 // P
FF1_HALF = FF1_TILES // 2
AQ, AK, BQ, BK, CQ, CK, AV, BV, CV = 0, 6, 12, 16, 17, 19, 21, 27, 28
N_QKV = 30
REV_TILES = list(range(AQ, AQ + 6)) + list(range(BQ, BQ + 4))

LAYERS = 2
FF2_TILES = 2816 // P
RQ, RK, DQ, DK, RV, DV, RG = 0, 4, 8, 12, 16, 20, 24
N_MIX = 28
RET_HEADS = DIFF_HEADS = 4

U_QKV = 0
U_MERGE = U_QKV + N_QKV
U_OUT1 = U_MERGE + 4 * KT
U_FF1 = U_OUT1 + KT
UNITS_FF1_HALF = 2 * FF1_HALF + 2 * KT
U_B2 = U_FF1 + 2 * UNITS_FF1_HALF
UNITS_FF2 = 2 * FF2_TILES + 3 * KT
UNITS_LAYER = 2 * UNITS_FF2 + N_MIX + KT
N_UNITS = U_B2 + LAYERS * UNITS_LAYER
N_STREAM = N_UNITS + 2

G_QKV = 0
G_GATE = G_QKV + N_QKV
G_OUT1 = G_GATE + 3 * KT
G_FF1 = G_OUT1 + KT
GROUPS_FF1_HALF = 2 * FF1_HALF + KT
G_B2 = G_FF1 + 2 * GROUPS_FF1_HALF
GROUPS_FF2 = 2 * FF2_TILES + KT
GROUPS_LAYER = 2 * GROUPS_FF2 + N_MIX + KT

N_GAINS = 4 + 3 * LAYERS + 1

def _columns(sizes):
    at, out = 0, {}
    for name, n in sizes:
        out[name] = (at, n)
        at += n
    return out, at


PARAMS, N_PARAMS = _columns([
    ("gain", N_GAINS * KT), ("b_gate", 3 * KT), ("conv", 2 * FF1_TILES * 4), ("sinks", B_HEADS),
    ("gn", LAYERS * 4), ("subln", LAYERS), ("lams", LAYERS * 4 * HD),
    ("ident", P), ("ones", P), ("eps", 1), ("lam_init", LAYERS), ("one_minus_init", LAYERS),
])
CONST1, N_CONST1 = _columns([("tri", P), ("cmask", SEQ)])
N_DIST = SEQ + P
N_BUCKETS = 32
N_BIAS = 3 * A_HEADS + B_HEADS
BIAS_ROWS = N_BUCKETS + 4
CONST2, N_CONST2 = _columns([
    ("cos_r", T2), ("sin_r", T2), ("cos_d", T2), ("sin_d", T2),
    ("decay", RET_HEADS * P), ("q_decay", RET_HEADS * P), ("k_decay", RET_HEADS), ("k_decay_meta", RET_HEADS),
    ("dmask", P),
])


def program(nc, x_d, meta_d, stream_d, params_d, const1_d, const2_d, bias_lhs_d, bias_rhs_d, scratch, out_d):
    ctx = ExitStack()
    with ctx:
        def alloc(stack, name, shape, dt=F32):
            return stack.enter_context(nc.sbuf_tensor(name, shape, dt))

        def sem(name):
            return ctx.enter_context(nc.semaphore(name))

        xT = alloc(ctx, "xT", [P, KT, T2])
        h_hi = alloc(ctx, "h_hi", [P, KT, T2], F32R)
        h_lo = alloc(ctx, "h_lo", [P, KT, T2], F32R)
        w_raw = alloc(ctx, "w_raw", [P, 2, KT * P])
        w_hi = alloc(ctx, "w_hi", [P, 2, KT * P], F32R)
        w_lo = alloc(ctx, "w_lo", [P, 2, KT * P], F32R)
        tmp = alloc(ctx, "tmp", [P, 4, T2])
        sumsq = alloc(ctx, "sumsq", [P, T2])
        std = alloc(ctx, "std", [P, T2])
        rstd = alloc(ctx, "rstd", [P, T2])
        params = alloc(ctx, "params", [P, N_PARAMS])
        stat = alloc(ctx, "stat", [P, 64])
        neg_lam = alloc(ctx, "neg_lam", [P, LAYERS])
        subw = alloc(ctx, "subw", [P, LAYERS])

        def par(name):
            a, n = PARAMS[name]
            return params[:, a:a + n]

        gain = par("gain").rearrange("p (n k) -> p n k", k=KT)
        b_gate = par("b_gate").rearrange("p (n k) -> p n k", k=KT)
        conv = par("conv").rearrange("p (f c) -> p f c", c=4)
        sinks = par("sinks")
        gn_w = par("gn").rearrange("p (l h) -> p l h", h=4)
        ident, ones, eps = par("ident"), par("ones"), par("eps")
        lams = par("lams").rearrange("p (l a d) -> p l a d", a=4, d=HD)

        with ExitStack() as s:
            qkv = alloc(s, "qkv", [P, N_QKV, SEQ])
            bias_a0 = alloc(s, "bias_a0", [P, A_HEADS, 2 * P])
            bias_a = alloc(s, "bias_a", [P, 2, A_HEADS, SEQ])
            bias_b = alloc(s, "bias_b", [P, B_HEADS, 2 * P])
            logit = alloc(s, "logit", [P, 2, 1280])
            probT = alloc(s, "probT", [P, 2, 10, P])
            const1 = alloc(s, "const1", [P, N_CONST1])
        tri = const1[:, CONST1["tri"][0]:CONST1["tri"][0] + P]
        cmask = const1[:, CONST1["cmask"][0]:CONST1["cmask"][0] + SEQ]
        bias_lhs, bias_rhs = logit[0:BIAS_ROWS, 1, 1024:1024 + N_BIAS], logit[0:BIAS_ROWS, 0, 0:N_DIST]
        bias_vec = logit[0:N_BIAS, 1, 0:N_DIST]

        const2 = alloc(ctx, "const2", [P, N_CONST2])

        def con2(name):
            a, n = CONST2[name]
            return const2[:, a:a + n]

        with ExitStack() as s:
            y_merge = alloc(s, "y_merge", [P, KT, SEQ])
            o_hi = alloc(s, "o_hi", [P, KT, SEQ], F32R)
            o_lo = alloc(s, "o_lo", [P, KT, SEQ], F32R)
            m_hi = alloc(s, "m_hi", [P, KT, SEQ], F32R)
            m_lo = alloc(s, "m_lo", [P, KT, SEQ], F32R)
            sig = alloc(s, "sig", [P, 3, SEQ])
            prod = alloc(s, "prod", [P, 3, SEQ])

        with ExitStack() as s:
            y_ffn = alloc(s, "y_ffn", [P, KT, SEQ])
            f1_hi = alloc(s, "f1_hi", [P, FF1_HALF, SEQ], F32R)
            f1_lo = alloc(s, "f1_lo", [P, FF1_HALF, SEQ], F32R)
            u_pad = alloc(s, "u_pad", [P, 2, SEQ + 2])
            cv = alloc(s, "cv", [P, 2, SEQ])

        with ExitStack() as s:
            f2_hi = alloc(s, "f2_hi", [P, FF2_TILES, T2], F32R)
            f2_lo = alloc(s, "f2_lo", [P, FF2_TILES, T2], F32R)

        mix = alloc(ctx, "mix", [P, N_MIX, T2])
        v_meta = alloc(ctx, "v_meta", [META, 8, P])
        with ExitStack() as s:
            sd = alloc(s, "sd", [P, RET_HEADS, SEQ])
            sd_meta = alloc(s, "sd_meta", [META, RET_HEADS, META])
            state = alloc(s, "state", [P, RET_HEADS, NBLK, P])
            kd = alloc(s, "kd", [P, RET_HEADS, 3, P])
            kd_meta = alloc(s, "kd_meta", [META, RET_HEADS, P])
        with ExitStack() as s:
            e_prob = alloc(s, "e_prob", [P, 2, 2, T2])
            aT = alloc(s, "aT", [P, 2, SEQ])
            aT_meta = alloc(s, "aT_meta", [META, 2, P])
            rs = alloc(s, "rs", [P, 4, T2])

        ps = ctx.enter_context(nc.psum_tensor("ps", [P, 8, 512], F32))

        w_arrived = [sem("w_arrived0"), sem("w_arrived1")]
        hi_done, lo_done = sem("hi_done"), sem("lo_done")
        unit_done = sem("unit_done")
        slot_free = [sem("slot_free0"), sem("slot_free1")]
        small_in, x_in, meta_in, x_again = sem("small_in"), sem("x_in"), sem("meta_in"), sem("x_again")
        const1_in, const2_in = sem("const1_in"), sem("const2_in")
        bias_in, bias_ps, bias_vec_done = sem("bias_in"), sem("bias_ps"), sem("bias_vec_done")
        bias_out, bias_ready = sem("bias_out"), sem("bias_ready")
        lam_dot, lam_exp = sem("lam_dot"), sem("lam_exp")
        sumsq_done, stat_ps, std_done = sem("sumsq_done"), sem("stat_ps"), sem("std_done")
        h_tmp, h_hi_done, h_lo_done = sem("h_tmp"), sem("h_hi_done"), sem("h_lo_done")
        vt_done, vt_read = sem("vt_done"), sem("vt_read")
        s_done, l_done, p_done, r_done = sem("s_done"), sem("l_done"), sem("p_done"), sem("r_done")
        t_done, t_read = sem("t_done"), [sem("t_read0"), sem("t_read1")]
        cum_done, cum_read, wts_done = sem("cum_done"), sem("cum_read"), sem("wts_done")
        o_done, o_read = sem("o_done"), sem("o_read")
        oh_done, ol_done = sem("oh_done"), sem("ol_done")
        br_free, m_tmp, mh_done, ml_done = sem("br_free"), sem("m_tmp"), sem("mh_done"), sem("ml_done")
        conv_done, gelu_done = sem("conv_done"), sem("gelu_done")
        a_tmp, ah_done, al_done = sem("a_tmp"), sem("ah_done"), sem("al_done")
        swap_done = sem("swap_done")
        tp_done, tp_act, tp_dve = sem("tp_done"), sem("tp_act"), sem("tp_dve")
        sc_done, sd_done, st_done, state_done = sem("sc_done"), sem("sd_done"), sem("st_done"), sem("state_done")
        ro_done, ro_read, mu_done, cen_done = sem("ro_done"), sem("ro_read"), sem("mu_done"), sem("cen_done")
        sq_done, var_done, vstd_done = sem("sq_done"), sem("var_done"), sem("vstd_done")
        y_tmp, yh_done, yl_done = sem("y_tmp"), sem("yh_done"), sem("yl_done")
        f_s, f_max, f_exp, f_a, f_t = sem("f_s"), sem("f_max"), sem("f_exp"), sem("f_a"), sem("f_t")
        f_read, f_read_meta, f_o, f_o_read = sem("f_read"), sem("f_read_meta"), sem("f_o"), sem("f_o_read")
        f_sq, f_sum, f_std = sem("f_sq"), sem("f_sum"), sem("f_std")
        m0_done, carried = sem("m0_done"), sem("carried")
        y_out, y_sent = sem("y_out"), [sem("y_sent0"), sem("y_sent1")]

        def wait(eng, s, value):
            if not (isinstance(value, int) and value <= 0):
                eng.wait_ge(s, value)

        def at(i):
            return slice(i, i + 1) if isinstance(i, int) else bass.ds(i, 1)

        def tile(t, i, n):
            return t[:, at(i), 0:n].rearrange("p a n -> p (a n)")

        def halves(ap, n):
            return ap.rearrange("p (a n) -> p a n", a=1 if n == T1 else 2)

        def bank(b, n):
            return ps[:, b:b + 1, 0:T1] if n == T1 else ps[:, b:b + 2, 0:T2 // 2]

        def parts(n):
            return [(0, 0, T1)] if n == T1 else [(0, 0, T2 // 2), (1, T2 // 2, T2)]

        def following(half, s):
            return half + 1, s

        units1 = ([("A", h, b) for b in range(NBLK) for h in range(A_HEADS)]
                  + [("B", g, b) for b in range(NBLK) for g in range(2)]
                  + [("C", h, 0) for h in range(C_HEADS)])
        N1 = len(units1)

        def a_segments(h, b):
            out, place = [], 0
            for g in range(3):
                k0 = max(0, b - 1) * P if g == 0 else 0
                nk = (b + 1) * P - k0
                bias = bias_a0[:, h, 2 * P - nk:] if g == 0 else bias_a[:, g - 1, h, SEQ - nk:]
                t = 2 * g + h // 2
                out.append((g, k0, nk, place, bias, AQ + t, AK + t, AV + t))
                place += nk
            return out

        def a_width(h, b):
            return sum(x[2] for x in a_segments(h, b))

        def c_place(kb):
            return [(0, 0), (1, 0), (2, 0), (1, 384)][kb] + (SEQ - P * kb, [0, 512, 896, 1152][kb])

        def rev(b):
            return slice(SEQ - P * (b + 1), SEQ - P * b)

        def t_batches(unit):
            kind, h, b = unit
            if kind == "A":
                blocks = [(i * P, i) for i in range(a_width(h, b) // P)]
            elif kind == "B":
                nk = min(b + 1, 2) * P
                blocks = [(i * (nk + 1) + j * P, i * (nk // P) + j) for i in range(4) for j in range(nk // P)]
            else:
                blocks = []
            return [blocks[i:i + 4] for i in range(0, len(blocks), 4)]

        batch_at = [sum(len(t_batches(x)) for x in units1[:n]) for n in range(N1)]
        c_at = [sum(x[0] == "C" for x in units1[:n]) for n in range(N1)]

        diff_units = [(h, b) for b in [NBLK] + list(range(NBLK)) for h in range(DIFF_HEADS)]
        ND = len(diff_units)

        def d_cols(b):
            return (SEQ, META, 0) if b == NBLK else (P * b, P, P * (b + 1))

        tp_tiles = [RV + i for i in range(4)] + [DV + i for i in range(4)] + [RK + i for i in range(4)]
        NTP = len(tp_tiles)

        def ffn2_base(which, L):
            return (U_B2 // 2 + UNITS_LAYER // 2 * L + which * (UNITS_FF2 + N_MIX + KT) // 2,
                    G_B2 // 2 + GROUPS_LAYER // 2 * L + which * (GROUPS_FF2 + N_MIX + KT) // 2,
                    FF1_TILES + FF2_TILES * (2 * L + which))

        def mix_base(L):
            return (U_B2 + UNITS_FF2) // 2 + UNITS_LAYER // 2 * L, (G_B2 + GROUPS_FF2) // 2 + GROUPS_LAYER // 2 * L

        block = ctx.enter_context(nc.Block())

        @block.sync
        def _(sp):
            def send(i):
                for s in range(2):
                    wait(sp, lo_done, 2 * i + s - 1)
                    sp.dma_start(w_raw[:, s, :], stream_d[at(2 * i + s), :, :].rearrange("a p n -> (a p) n")
                                 ).then_inc(w_arrived[s], 16)
            send(0)
            with sp.Fori(1, N_STREAM // 2) as i:
                send(i)
            for s in range(2):
                sp.wait_ge(w_arrived[s], 16 * (N_STREAM // 2))

        @block.gpsimd
        def _(pool):
            pool.dma_start(params[:, :], params_d).then_inc(small_in, 16)
            pool.dma_start(xT[:, :, 0:SEQ], x_d).then_inc(x_in, 16)
            pool.dma_start(xT[:, :, SEQ:T2], meta_d).then_inc(meta_in, 16)
            pool.dma_start(bias_lhs, bias_lhs_d).then_inc(bias_in, 16)
            pool.dma_start(bias_rhs, bias_rhs_d).then_inc(bias_in, 16)
            pool.dma_start(const1[:, :], const1_d).then_inc(const1_in, 16)
            pool.wait_ge(bias_vec_done, 1)
            pool.dma_start(scratch, bias_vec).then_inc(bias_out, 16)
            pool.wait_ge(bias_out, 16)

            def hankel(vector, n_vectors, first, n):
                return bass.AP(tensor=scratch.tensor, offset=vector * N_DIST + first,
                               ap=[[1, P], [N_DIST, n_vectors], [1, n]])

            pool.dma_start(bias_a0[:, :, :], hankel(0, A_HEADS, 2 * P, 2 * P)).then_inc(bias_ready, 16)
            pool.dma_start(bias_a[:, 0, :, :], hankel(A_HEADS, A_HEADS, 0, SEQ)).then_inc(bias_ready, 16)
            pool.dma_start(bias_a[:, 1, :, :], hankel(2 * A_HEADS, A_HEADS, 0, SEQ)).then_inc(bias_ready, 16)
            pool.dma_start(bias_b[:, :, :], hankel(3 * A_HEADS, B_HEADS, 2 * P, 2 * P)).then_inc(bias_ready, 16)
            pool.wait_ge(ol_done, 2)
            pool.dma_start(xT[:, :, 0:SEQ], x_d).then_inc(x_again, 16)
            pool.dma_start(const2[:, :], const2_d).then_inc(const2_in, 16)
            for k in range(KT):
                pool.wait_ge(y_out, k + 1)
                pool.dma_start(out_d[k, :, :], tmp[:, k % 2, 0:SEQ]).then_inc(y_sent[k % 2], 16)
            for s in range(2):
                pool.wait_ge(y_sent[s], 16 * KT // 2)

        @block.scalar
        def _(act):
            def split_hi(half, s):
                act.wait_ge(w_arrived[s], 16 * half + 16)
                wait(act, unit_done, 2 * half + s - 1)
                nc.scalar.activation(w_hi[:, s, :], w_raw[:, s, :], ACT.Copy).then_inc(hi_done, 1)

            def stat_root(r, n):
                act.wait_ge(stat_ps, r + 1)
                nc.scalar.activation(halves(std[:, 0:n], n), bank(4, n), ACT.Sqrt, bias=eps,
                                     scale=1.0 / DM).then_inc(std_done, 1)

            def h_upper(q, n):
                for k in range(KT):
                    act.wait_ge(h_tmp, KT * q + k + 1)
                    nc.scalar.activation(h_hi[:, k, 0:n], tmp[:, k % 4, 0:n], ACT.Copy).then_inc(h_hi_done, 1)

            split_hi(0, 0)
            split_hi(0, 1)
            act.wait_ge(bias_ps, 1)
            nc.scalar.activation(bias_vec.rearrange("p (a n) -> p a n", a=2), ps[0:N_BIAS, 6:8, 0:N_DIST // 2],
                                 ACT.Copy).then_inc(bias_vec_done, 1)
            act.wait_ge(lam_dot, 1)
            nc.scalar.activation(stat[:, 4:8], stat[:, 0:4], ACT.Exp).then_inc(lam_exp, 1)
            stat_root(0, T1)
            h_upper(0, T1)

            def qkv_out(i, reverse):
                for s in range(2):
                    split_hi(*following(i, s))
                    act.wait_ge(unit_done, 2 * i + s + 1)
                    src = ps[:, 2 * s, ::-1] if reverse else ps[:, 2 * s, :]
                    nc.scalar.activation(tile(qkv, 2 * i + s, SEQ), src, ACT.Copy).then_inc(slot_free[s], 1)

            qkv_out(0, True)
            for first, end, reverse in ((AQ + 2, AK, True), (AK, BQ, False), (BQ, BK, True), (BK, N_QKV, False)):
                with act.Fori(first // 2, end // 2) as i:
                    qkv_out(i, reverse)

            def exps(n):
                kind, h, b = units1[n]
                s = n % 2
                act.wait_ge(l_done, n + 1)
                if kind == "A":
                    row = logit[:, s, 0:a_width(h, b)]
                    nc.scalar.activation(row, row, ACT.Exp, bias=stat[:, 8 + 4 * s:9 + 4 * s],
                                         accum_out=stat[:, 16 + 4 * s:17 + 4 * s]).then_inc(p_done, 1)
                elif kind == "B":
                    nk = min(b + 1, 2) * P + 1
                    for j in range(4):
                        row = logit[:, s, j * nk:(j + 1) * nk]
                        last = nc.scalar.activation(row, row, ACT.Exp, bias=stat[:, 8 + 4 * s + j:9 + 4 * s + j],
                                                    accum_out=stat[:, 16 + 4 * s + j:17 + 4 * s + j])
                    last.then_inc(p_done, 1)
                else:
                    soft = probT[:, s, :, :].rearrange("p a n -> p (a n)")
                    act.wait_ge(o_done, n - 1)
                    nc.scalar.activation(soft, logit[:, s, :], ACT.Abs)
                    act.drain()
                    nc.scalar.activation(soft, soft, ACT.Exp, scale=-1.0)
                    act.drain()
                    nc.scalar.activation(soft, soft, ACT.Ln, bias=1.0).then_inc(p_done, 1)

            exps(0)
            for n, (kind, h, b) in enumerate(units1):
                s = n % 2
                for j, blocks in enumerate(t_batches(units1[n])):
                    bt = batch_at[n] + j
                    act.wait_ge(t_done, bt + 1)
                    first, k = blocks[0][1], len(blocks)
                    nc.scalar.activation(probT[:, s, first:first + k, :],
                                         ps[:, 6 + bt % 2, 0:k * P].rearrange("p (a n) -> p a n", n=P),
                                         ACT.Copy).then_inc(t_read[bt % 2], 1)
                if kind == "C":
                    act.wait_ge(cum_read, c_at[n] + 1)
                    nc.scalar.activation(logit[:, s, :], logit[:, s, :], ACT.Exp).then_inc(wts_done, 1)
                if n + 1 < N1:
                    exps(n + 1)
                act.wait_ge(o_done, n + 1)
                if kind == "A":
                    lo = HD * (h % 2)
                    dst, src = xT[lo:lo + HD, h // 2, P * b:P * (b + 1)][:, ::-1], ps[lo:lo + HD, 3 * s, 0:P]
                elif kind == "B":
                    lo = HD * h
                    dst = xT[lo:lo + HD, 2:6, P * b:P * (b + 1)][:, :, ::-1]
                    src = ps[lo:lo + HD, 3 * s, :].rearrange("p (a n) -> p a n", n=P)
                else:
                    lo = HD * (h % 2)
                    dst, src = xT[lo:lo + HD, 6 + h // 2, 0:SEQ], ps[lo:lo + HD, 3 * s, :]
                nc.scalar.activation(dst, src, ACT.Copy).then_inc(o_read, 1)
            act.wait_ge(o_read, N1)
            for j in range(2):
                nc.scalar.activation(o_hi[:, 4 * j:4 * j + 4, :], xT[:, 4 * j:4 * j + 4, 0:SEQ],
                                     ACT.Copy).then_inc(oh_done, 1)

            with act.Fori(0, KT // 2) as i:
                for odd in range(2):
                    m = 2 * i + odd
                    for n in range(3):
                        split_hi(*following(U_MERGE // 2 + 4 * i + 2 * odd + n // 2, n % 2))
                        s = (odd + n) % 2
                        act.wait_ge(unit_done, U_MERGE + 4 * m + n + 1)
                        nc.scalar.activation(sig[:, n, :], ps[:, 2 * s, :], ACT.Sigmoid,
                                             bias=b_gate[:, n, at(m)]).then_inc(slot_free[s], 1)
                    split_hi(*following(U_MERGE // 2 + 4 * i + 2 * odd + 1, 1))
                    act.wait_ge(m_tmp, m + 1)
                    nc.scalar.activation(tile(m_hi, m, SEQ), prod[:, 0, :], ACT.Copy).then_inc(mh_done, 1)

            with act.Fori(0, KT // 2) as i:
                for s in range(2):
                    split_hi(*following(U_OUT1 // 2 + i, s))
                    act.wait_ge(unit_done, U_OUT1 + 2 * i + s + 1)
                    nc.scalar.activation(tile(y_merge, 2 * i + s, SEQ), ps[:, 2 * s, :], ACT.Copy
                                         ).then_inc(slot_free[s], 1)
            stat_root(1, T1)
            stat_root(2, T1)
            h_upper(1, T1)

            for part in range(2):
                u0 = U_FF1 + UNITS_FF1_HALF * part
                with act.Fori(0, FF1_HALF) as j:
                    jj = FF1_HALF * part + j
                    for s in range(2):
                        split_hi(*following(u0 // 2 + j, s))
                        act.wait_ge(unit_done, u0 + 2 * j + s + 1)
                        nc.scalar.activation(u_pad[:, s, 2:], ps[:, 2 * s, :], ACT.Copy)
                        nc.scalar.activation(cv[:, s, :], ps[:, 2 * s, :], ACT.Identity,
                                             scale=conv[:, at(jj + FF1_TILES * s), 2],
                                             bias=conv[:, at(jj + FF1_TILES * s), 3]).then_inc(slot_free[s], 1)
                    act.wait_ge(conv_done, 2 * jj + 1)
                    nc.scalar.activation(tmp[:, 0, 0:SEQ], cv[:, 0, :], ACT.Gelu_apprx_tanh).then_inc(gelu_done, 1)
                    act.wait_ge(a_tmp, jj + 1)
                    nc.scalar.activation(tile(f1_hi, j, SEQ), tmp[:, 1, 0:SEQ], ACT.Copy).then_inc(ah_done, 1)
                with act.Fori(0, KT) as m:
                    for s in range(2):
                        split_hi(*following(u0 // 2 + FF1_HALF + m, s))
            stat_root(3, T1)

            def ffn2(which, L):
                u0, g0, a0 = ffn2_base(which, L)
                with act.Fori(0, FF2_TILES) as j:
                    split_hi(*following(u0 + j, 0))
                    act.wait_ge(unit_done, 2 * (u0 + j) + 1)
                    nc.scalar.activation(halves(tmp[:, 0, :], T2), bank(0, T2), ACT.Silu).then_inc(slot_free[0], 1)
                    split_hi(*following(u0 + j, 1))
                    act.wait_ge(slot_free[1], g0 + j + 1)
                    nc.scalar.activation(tile(f2_hi, j, T2), tmp[:, 1, :], ACT.Copy).then_inc(ah_done, 1)
                with act.Fori(0, KT // 2) as i:
                    for n in range(6):
                        split_hi(*following(u0 + FF2_TILES + 3 * i + n // 2, n % 2))

            def mixer(L):
                u0, g0 = mix_base(L)
                for first, step in ((RQ, 64), (DQ, 32)):
                    with act.Fori(first // 2, first // 2 + 4) as i:
                        for s in range(2):
                            split_hi(*following(u0 + i, s))
                            act.wait_ge(unit_done, 2 * (u0 + i) + s + 1)
                            act.wait_ge(slot_free[s], g0 + i)
                            for lo in range(0, P, step):
                                other = lo ^ step
                                last = nc.scalar.activation(halves(tmp[lo:lo + step, s, :], T2),
                                                            bank(2 * s, T2)[other:other + step], ACT.Copy)
                            last.then_inc(swap_done, 1)
                for first, end, func in ((RV, RG, ACT.Copy), (RG, N_MIX, ACT.Silu)):
                    with act.Fori(first // 2, end // 2) as i:
                        for s in range(2):
                            split_hi(*following(u0 + i, s))
                            act.wait_ge(unit_done, 2 * (u0 + i) + s + 1)
                            nc.scalar.activation(halves(tile(mix, 2 * i + s, T2), T2), bank(2 * s, T2), func
                                                 ).then_inc(slot_free[s], 1)
                for t in range(8):
                    act.wait_ge(tp_done, NTP * L + t + 1)
                    nc.scalar.activation(mix[:, tp_tiles[t], 0:SEQ], ps[:, 4 + t % 2, :], ACT.Copy).then_inc(tp_act, 1)
                for h in range(RET_HEADS):
                    act.wait_ge(ro_done, 4 * L + h + 1)
                    nc.scalar.activation(mix[:, RK + h, 0:SEQ], ps[:, 4 + h, :], ACT.Copy)
                    nc.scalar.activation(mix[:, RK + h, SEQ:T2], ps[:, h, 0:META], ACT.Copy).then_inc(ro_read, 1)
                for h in range(RET_HEADS):
                    act.wait_ge(cen_done, 4 * L + h + 1)
                    nc.scalar.activation(tmp[:, h, :], mix[:, RK + h, :], ACT.Square).then_inc(sq_done, 1)
                for h in range(RET_HEADS):
                    act.wait_ge(var_done, 4 * L + h + 1)
                    nc.scalar.activation(halves(rs[:, h, :], T2), bank(2 * h, T2), ACT.Sqrt, bias=eps,
                                         scale=1.0 / P).then_inc(vstd_done, 1)
                for h in range(RET_HEADS):
                    act.wait_ge(y_tmp, 8 * L + h + 1)
                    nc.scalar.activation(h_hi[:, h, :], mix[:, RK + h, :], ACT.Copy).then_inc(yh_done, 1)

                def d_exps(n):
                    h, b = diff_units[n]
                    s = n % 2
                    q0, nq, nk = d_cols(b)
                    act.wait_ge(f_max, ND * L + n + 1)
                    for m in range(2):
                        shift = stat[0:nq, 8 + 4 * s + m:9 + 4 * s + m]
                        if nk:
                            nc.scalar.activation(e_prob[:, s, m, 0:nk], ps[:, 3 * s + m, 0:nk], ACT.Exp, bias=shift,
                                                 scale=SCALE, accum_out=stat[:, 16 + 4 * s + m:17 + 4 * s + m])
                        last = nc.scalar.activation(e_prob[0:nq, s, m, nk:nk + META],
                                                    ps[0:nq, 3 * s + 2, META * m:META * (m + 1)], ACT.Exp, bias=shift,
                                                    scale=SCALE, accum_out=stat[0:nq, 18 + 4 * s + m:19 + 4 * s + m])
                    last.then_inc(f_exp, 1)

                d_exps(0)
                for n, (h, b) in enumerate(diff_units):
                    s = n % 2
                    q0, nq, nk = d_cols(b)
                    act.wait_ge(f_t, ND * L + n + 1)
                    if nk:
                        nc.scalar.activation(aT[:, s, 0:nk], ps[:, 6, 0:nk], ACT.Copy).then_inc(f_read, 1)
                    nc.scalar.activation(aT_meta[:, s, 0:nq], ps[0:META, 7, 0:nq], ACT.Copy).then_inc(f_read_meta, 1)
                    if n + 1 < ND:
                        d_exps(n + 1)
                    act.wait_ge(f_o, ND * L + n + 1)
                    nc.scalar.activation(mix[:, DQ + h, q0:q0 + nq], ps[:, 3 * s, 0:nq], ACT.Copy).then_inc(f_o_read, 1)
                for h in range(DIFF_HEADS):
                    act.wait_ge(f_o_read, ND * (L + 1))
                    nc.scalar.activation(tmp[:, h, :], mix[:, DQ + h, :], ACT.Square).then_inc(f_sq, 1)
                for h in range(DIFF_HEADS):
                    act.wait_ge(f_sum, 4 * L + h + 1)
                    nc.scalar.activation(halves(rs[:, h, :], T2), bank(2 * h, T2), ACT.Sqrt, bias=eps,
                                         scale=1.0 / P).then_inc(f_std, 1)
                for h in range(DIFF_HEADS):
                    act.wait_ge(y_tmp, 8 * L + 4 + h + 1)
                    nc.scalar.activation(h_hi[:, 4 + h, :], mix[:, DQ + h, :], ACT.Copy).then_inc(yh_done, 1)
                with act.Fori(N_MIX // 2, (N_MIX + KT) // 2) as i:
                    for s in range(2):
                        split_hi(*following(u0 + i, s))

            with act.Fori(0, LAYERS) as L:
                for which in range(2):
                    stat_root(4 + 3 * L + 2 * which, T2)
                    h_upper(2 + 3 * L + 2 * which, T2)
                    ffn2(which, L)
                    if which == 0:
                        stat_root(5 + 3 * L, T2)
                        h_upper(3 + 3 * L, T2)
                        mixer(L)
            stat_root(4 + 3 * LAYERS, T2)

        @block.vector
        def _(dve):
            V = nc.vector

            def split_lo(half, s):
                dve.wait_ge(hi_done, 2 * half + s + 1)
                V.tensor_tensor(w_lo[:, s, :], w_raw[:, s, :], w_hi[:, s, :].bitcast(F32), ALU.subtract
                                ).then_inc(lo_done, 1)

            def stat_inverse(r, n):
                dve.wait_ge(std_done, r + 1)
                V.reciprocal(rstd[:, 0:n], std[:, 0:n])
                dve.drain()

            def h_lower(q, gain_at, n):
                for k in range(KT + 2):
                    if 4 <= k < KT:
                        dve.wait_ge(h_lo_done, KT * q + k - 3)
                    if k < KT:
                        V.scalar_tensor_tensor(tmp[:, k % 4, 0:n], xT[:, k, 0:n], gain[:, at(gain_at), k],
                                               rstd[:, 0:n], ALU.mult, ALU.mult).then_inc(h_tmp, 1)
                    if k >= 2:
                        dve.wait_ge(h_hi_done, KT * q + k - 1)
                        V.tensor_tensor(h_lo[:, k - 2, 0:n], tmp[:, (k - 2) % 4, 0:n],
                                        h_hi[:, k - 2, 0:n].bitcast(F32), ALU.subtract).then_inc(h_lo_done, 1)

            def add_square(src, n, inc=None):
                V.tensor_tensor(tmp[:, 3, 0:n], src, src, ALU.mult)
                dve.drain()
                last = V.tensor_tensor(sumsq[:, 0:n], sumsq[:, 0:n], tmp[:, 3, 0:n], ALU.add)
                if inc is not None:
                    last.then_inc(inc, 1)

            def add_normed(y, gain_at, n):
                V.memset(sumsq[:, 0:n], 0.0)
                for k in range(KT + 3):
                    if 0 <= k - 3 < KT:
                        V.tensor_tensor(sumsq[:, 0:n], sumsq[:, 0:n], tmp[:, 2 + (k - 3) % 2, 0:n], ALU.add)
                    if 0 <= k - 2 < KT:
                        V.tensor_tensor(tmp[:, 2 + (k - 2) % 2, 0:n], xT[:, k - 2, 0:n], xT[:, k - 2, 0:n], ALU.mult)
                    if 0 <= k - 1 < KT:
                        V.tensor_tensor(xT[:, k - 1, 0:n], xT[:, k - 1, 0:n], tmp[:, (k - 1) % 2, 0:n], ALU.add)
                    if k < KT:
                        V.scalar_tensor_tensor(tmp[:, k % 2, 0:n], y[:, k, 0:n], gain[:, at(gain_at), k],
                                               rstd[:, 0:n], ALU.mult, ALU.mult)
                    dve.drain()

            dve.wait_ge(small_in, 16)
            pair = tmp[:, 0, 0:LAYERS * 2 * HD].rearrange("p (l a d) -> p l a d", a=2, d=HD)
            for l in range(LAYERS):
                V.tensor_tensor(pair[:, l, :, :], lams[:, l, 0::2, :], lams[:, l, 1::2, :], ALU.mult)
            dve.drain()
            V.tensor_reduce(stat[:, 0:4].rearrange("p (l a) -> p l a", a=2), pair, AX.X, ALU.add).then_inc(lam_dot, 1)
            split_lo(0, 0)
            split_lo(0, 1)
            dve.wait_ge(lam_exp, 1)
            V.tensor_tensor(neg_lam[:, :], stat[:, 5:8:2], stat[:, 4:8:2], ALU.subtract)
            dve.drain()
            V.tensor_tensor(neg_lam[:, :], neg_lam[:, :], par("lam_init"), ALU.subtract)
            V.tensor_tensor(subw[:, :], par("subln"), par("one_minus_init"), ALU.mult)
            V.memset(sumsq[:, :], 0.0)
            dve.wait_ge(x_in, 16)
            for k in range(KT):
                dve.drain()
                add_square(xT[:, k, 0:SEQ], SEQ, sumsq_done if k == KT - 1 else None)
            stat_inverse(0, T1)
            h_lower(0, 0, T1)

            with dve.Fori(0, N_QKV // 2) as i:
                for s in range(2):
                    split_lo(*following(i, s))

            for t in range(9):
                dve.wait_ge(vt_done, t + 1)
                V.tensor_copy(qkv[:, AV + t, :], ps[:, 4 + t % 4, :]).then_inc(vt_read, 1)
            dve.wait_ge(bias_ready, 64)
            dve.wait_ge(const1_in, 16)

            def logits(n):
                kind, h, b = units1[n]
                s = n % 2
                dve.wait_ge(s_done, n + 1)
                wait(dve, o_done, n - 1)
                if kind == "A":
                    for g, k0, nk, place, bias, *_ in a_segments(h, b):
                        V.scalar_tensor_tensor(logit[:, s, place:place + nk], ps[:, 3 * s + g, 0:nk], SCALE, bias,
                                               ALU.mult, ALU.add)
                    dve.drain()
                    V.tensor_reduce(stat[:, 8 + 4 * s:9 + 4 * s], logit[:, s, 0:a_width(h, b)], AX.X, ALU.max,
                                    negate=True).then_inc(l_done, 1)
                elif kind == "B":
                    nk = min(b + 1, 2) * P
                    rows = logit[:, s, 0:4 * (nk + 1)].rearrange("p (a n) -> p a n", n=nk + 1)
                    src = ps[:, 3 * s:3 * s + 2, :].rearrange("p a (c n) -> p (a c) n", n=2 * P)[:, :, 0:nk]
                    V.scalar_tensor_tensor(rows[:, :, 0:nk], src, SCALE, bias_b[:, 4 * h:4 * h + 4, 2 * P - nk:],
                                           ALU.mult, ALU.add)
                    V.tensor_copy(rows[:, :, nk], sinks[:, 4 * h:4 * h + 4])
                    dve.drain()
                    V.tensor_reduce(stat[:, 8 + 4 * s:12 + 4 * s], rows, AX.X, ALU.max, negate=True).then_inc(l_done, 1)
                else:
                    for kb in range(NBLK):
                        bk, col, nq, place = c_place(kb)
                        last = V.scalar_tensor_tensor(logit[:, s, place:place + nq], ps[:, 3 * s + bk, col:col + nq],
                                                      SCALE, cmask[:, 0:nq], ALU.mult, ALU.add)
                    last.then_inc(l_done, 1)

            logits(0)
            for n, (kind, h, b) in enumerate(units1):
                s = n % 2
                dve.wait_ge(p_done, n + 1)
                rec = stat[:, 24 + 4 * s:28 + 4 * s]
                if kind == "A":
                    V.reciprocal(rec[:, 0:1], stat[:, 16 + 4 * s:17 + 4 * s])
                    dve.drain()
                    row = logit[:, s, 0:a_width(h, b)]
                    V.tensor_scalar(row, row, rec[:, 0:1], None, ALU.mult).then_inc(r_done, 1)
                elif kind == "B":
                    V.reciprocal(rec, stat[:, 16 + 4 * s:20 + 4 * s])
                    dve.drain()
                    nk = min(b + 1, 2) * P + 1
                    for j in range(4):
                        row = logit[:, s, j * nk:(j + 1) * nk - 1]
                        last = V.tensor_scalar(row, row, rec[:, j:j + 1], None, ALU.mult)
                    last.then_inc(r_done, 1)
                else:
                    soft = probT[:, s, :, :].rearrange("p a n -> p (a n)")
                    V.scalar_tensor_tensor(soft, logit[:, s, :], 0.0, soft, ALU.max, ALU.add).then_inc(r_done, 1)
                if n + 1 < N1:
                    logits(n + 1)
                if kind == "C":
                    dve.wait_ge(cum_done, c_at[n] + 1)
                    for kb in range(NBLK):
                        bk, col, nq, place = c_place(kb)
                        row = logit[:, s, place:place + nq]
                        last = V.tensor_tensor(row, row, ps[:, 3 * s + bk, col:col + nq], ALU.subtract)
                    last.then_inc(cum_read, 1)
            for j in range(2):
                dve.wait_ge(oh_done, j + 1)
                V.tensor_tensor(o_lo[:, 4 * j:4 * j + 4, :], xT[:, 4 * j:4 * j + 4, 0:SEQ],
                                o_hi[:, 4 * j:4 * j + 4, :].bitcast(F32), ALU.subtract).then_inc(ol_done, 1)
            dve.sem_inc(br_free, 1)

            with dve.Fori(0, KT // 2) as i:
                for odd in range(2):
                    m = 2 * i + odd
                    for n in range(4):
                        split_lo(*following(U_MERGE // 2 + 4 * i + 2 * odd + n // 2, n % 2))
                    dve.wait_ge(unit_done, U_MERGE + 4 * m + 4)
                    s = odd
                    dve.wait_ge(slot_free[s], G_GATE // 2 + 3 * i + 2 * odd + (1 - odd) + 1)
                    V.tensor_tensor(prod[:, :, :], sig[:, :, :], ps[:, 4:7, :], ALU.mult).then_inc(br_free, 1)
                    dve.drain()
                    V.tensor_tensor(prod[:, 0, :], prod[:, 0, :], prod[:, 1, :], ALU.add)
                    dve.drain()
                    V.tensor_tensor(prod[:, 0, :], prod[:, 0, :], prod[:, 2, :], ALU.add).then_inc(m_tmp, 1)
                    dve.wait_ge(mh_done, m + 1)
                    V.tensor_tensor(tile(m_lo, m, SEQ), prod[:, 0, :], tile(m_hi, m, SEQ).bitcast(F32), ALU.subtract
                                    ).then_inc(ml_done, 1)

            V.memset(sumsq[:, :], 0.0)
            with dve.Fori(0, KT // 2) as i:
                for s in range(2):
                    split_lo(*following(U_OUT1 // 2 + i, s))
                    dve.drain()
                    dve.wait_ge(slot_free[s], G_OUT1 // 2 + i + 1)
                    add_square(tile(y_merge, 2 * i + s, SEQ), SEQ)
            dve.drain()
            dve.sem_inc(sumsq_done, 1)
            stat_inverse(1, T1)
            dve.wait_ge(x_again, 16)
            add_normed(y_merge, 1, SEQ)
            dve.sem_inc(sumsq_done, 1)
            stat_inverse(2, T1)
            h_lower(1, 2, T1)

            V.memset(u_pad[:, :, 0:2], 0.0)
            dve.drain()
            for part in range(2):
                u0 = U_FF1 + UNITS_FF1_HALF * part
                g0 = G_FF1 + GROUPS_FF1_HALF * part
                with dve.Fori(0, FF1_HALF) as j:
                    jj = FF1_HALF * part + j
                    for s in range(2):
                        split_lo(*following(u0 // 2 + j, s))
                        dve.wait_ge(slot_free[s], g0 // 2 + j + 1)
                        V.scalar_tensor_tensor(cv[:, s, :], u_pad[:, s, 1:SEQ + 1], conv[:, at(jj + FF1_TILES * s), 1],
                                               cv[:, s, :], ALU.mult, ALU.add)
                        dve.drain()
                        V.scalar_tensor_tensor(cv[:, s, :], u_pad[:, s, 0:SEQ], conv[:, at(jj + FF1_TILES * s), 0],
                                               cv[:, s, :], ALU.mult, ALU.add).then_inc(conv_done, 1)
                    dve.drain()
                    dve.wait_ge(gelu_done, jj + 1)
                    V.tensor_tensor(tmp[:, 1, 0:SEQ], tmp[:, 0, 0:SEQ], cv[:, 1, :], ALU.mult).then_inc(a_tmp, 1)
                    dve.wait_ge(ah_done, jj + 1)
                    V.tensor_tensor(tile(f1_lo, j, SEQ), tmp[:, 1, 0:SEQ], tile(f1_hi, j, SEQ).bitcast(F32),
                                    ALU.subtract).then_inc(al_done, 1)
                if part == 1:
                    V.memset(sumsq[:, :], 0.0)
                with dve.Fori(0, KT // 2) as i:
                    for s in range(2):
                        m = 2 * i + s
                        split_lo(*following(u0 // 2 + FF1_HALF + m, 0))
                        split_lo(*following(u0 // 2 + FF1_HALF + m, 1))
                        dve.wait_ge(unit_done, u0 + 2 * FF1_HALF + 2 * m + 2)
                        y = tile(y_ffn, m, SEQ)
                        if part == 0:
                            V.tensor_copy(y, ps[:, 2 * s, :]).then_inc(slot_free[s], 1)
                        else:
                            V.tensor_tensor(y, y, ps[:, 2 * s, :], ALU.add).then_inc(slot_free[s], 1)
                            dve.drain()
                            add_square(y, SEQ)
                            dve.drain()
                dve.drain()
            dve.sem_inc(sumsq_done, 1)
            stat_inverse(3, T1)
            add_normed(y_ffn, 3, SEQ)
            dve.wait_ge(meta_in, 16)
            square = tmp[:, 0, 0:KT * META].rearrange("p (k n) -> p k n", n=META)
            V.tensor_tensor(square, xT[:, :, SEQ:T2], xT[:, :, SEQ:T2], ALU.mult)
            dve.drain()
            V.tensor_reduce(sumsq[:, SEQ:T2], square.rearrange("p k n -> p n k"), AX.X, ALU.add).then_inc(sumsq_done, 1)
            dve.wait_ge(const2_in, 16)

            def ffn2(which, L):
                u0, g0, a0 = ffn2_base(which, L)
                with dve.Fori(0, FF2_TILES) as j:
                    split_lo(*following(u0 + j, 0))
                    split_lo(*following(u0 + j, 1))
                    dve.drain()
                    dve.wait_ge(unit_done, 2 * (u0 + j) + 2)
                    dve.wait_ge(slot_free[0], g0 + j + 1)
                    V.tensor_tensor(halves(tmp[:, 1, :], T2), halves(tmp[:, 0, :], T2), bank(2, T2), ALU.mult
                                    ).then_inc(slot_free[1], 1)
                    dve.wait_ge(ah_done, a0 + j + 1)
                    V.tensor_tensor(tile(f2_lo, j, T2), tmp[:, 1, :], tile(f2_hi, j, T2).bitcast(F32), ALU.subtract
                                    ).then_inc(al_done, 1)
                V.memset(sumsq[:, :], 0.0)
                with dve.Fori(0, KT // 2) as i:
                    for s in range(2):
                        for n in range(3):
                            c = 3 * s + n
                            split_lo(*following(u0 + FF2_TILES + 3 * i + c // 2, c % 2))
                        dve.wait_ge(unit_done, 2 * (u0 + FF2_TILES) + 6 * i + 3 * s + 3)
                        x = tile(xT, 2 * i + s, T2)
                        V.scalar_tensor_tensor(halves(x, T2), bank(2 * s, T2), 0.5, halves(x, T2), ALU.mult, ALU.add
                                               ).then_inc(slot_free[s], 1)
                        dve.drain()
                        add_square(x, T2)
                        dve.drain()
                dve.sem_inc(sumsq_done, 1)

            def mixer(L):
                u0, g0 = mix_base(L)
                for first, tab in ((RQ, "r"), (DQ, "d")):
                    with dve.Fori(first // 2, first // 2 + 4) as i:
                        for s in range(2):
                            split_lo(*following(u0 + i, s))
                            dve.wait_ge(swap_done, 16 * L + 2 * i + s + 1)
                            x = tile(mix, 2 * i + s, T2)
                            V.tensor_tensor(halves(x, T2), bank(2 * s, T2), halves(con2("cos_" + tab), T2), ALU.mult)
                            V.tensor_tensor(tmp[:, s, :], tmp[:, s, :], con2("sin_" + tab), ALU.mult)
                            dve.drain()
                            V.tensor_tensor(x, x, tmp[:, s, :], ALU.add).then_inc(slot_free[s], 1)
                with dve.Fori(RV // 2, N_MIX // 2) as i:
                    for s in range(2):
                        split_lo(*following(u0 + i, s))
                for t in range(NTP):
                    dve.wait_ge(tp_done, NTP * L + t + 1)
                    if t < 8:
                        V.tensor_copy(v_meta[:, t, :], ps[0:META, 6 + t % 2, 0:P]).then_inc(tp_dve, 1)
                    else:
                        h = t - 8
                        V.tensor_scalar(kd[:, h, :, :], ps[:, 4 + t % 2, 0:3 * P].rearrange("p (a n) -> p a n", n=P),
                                        con2("k_decay")[:, h:h + 1], None, ALU.mult)
                        V.tensor_scalar(kd_meta[:, h, :], ps[0:META, 6 + t % 2, 0:P],
                                        con2("k_decay_meta")[0:META, h:h + 1], None, ALU.mult).then_inc(tp_dve, 1)
                decay = con2("decay").rearrange("p (h n) -> p h n", n=P)
                q_decay = con2("q_decay").rearrange("p (h n) -> p h n", n=P)

                def by_chunk(ap):
                    return ap.rearrange("p (a n) -> p a n", n=P)

                def each_chunk(ap):
                    return ap.unsqueeze(1).broadcast_to([P, NBLK, P])

                for h in range(RET_HEADS):
                    dve.wait_ge(sc_done, 4 * L + h + 1)
                    V.tensor_tensor(by_chunk(sd[:, h, :]), by_chunk(ps[:, h, :]), each_chunk(decay[:, h, :]), ALU.mult)
                    V.tensor_tensor(sd_meta[:, h, :], ps[0:META, 4 + h, 0:META], decay[0:META, h, 0:META], ALU.mult)
                    q = by_chunk(mix[:, RQ + h, 0:SEQ])
                    V.tensor_tensor(q, q, each_chunk(q_decay[:, h, :]), ALU.mult).then_inc(sd_done, 1)
                dve.wait_ge(st_done, 4 * (L + 1))
                for n in range(NBLK):
                    for h in range(RET_HEADS):
                        if n == 0:
                            V.tensor_copy(state[:, h, 0, :], ps[:, h, 0:P])
                        else:
                            chunk_decay = (1.0 - 2.0 ** (-5.0 - h)) ** P
                            V.scalar_tensor_tensor(state[:, h, n, :], state[:, h, n - 1, :], chunk_decay,
                                                   ps[:, h, n * P:(n + 1) * P], ALU.mult, ALU.add)
                    dve.drain()
                dve.sem_inc(state_done, 1)
                for h in range(RET_HEADS):
                    dve.wait_ge(mu_done, 4 * L + h + 1)
                    o = halves(mix[:, RK + h, :], T2)
                    V.scalar_tensor_tensor(o, bank(2 * h, T2), -1.0 / P, o, ALU.mult, ALU.add).then_inc(cen_done, 1)
                for h in range(RET_HEADS):
                    o = mix[:, RK + h, :]
                    dve.wait_ge(vstd_done, 4 * L + h + 1)
                    V.reciprocal(rs[:, h, :], rs[:, h, :])
                    dve.drain()
                    V.scalar_tensor_tensor(o, o, gn_w[:, at(L), h], rs[:, h, :], ALU.mult, ALU.mult)
                    dve.drain()
                    V.tensor_tensor(o, o, mix[:, RG + h, :], ALU.mult).then_inc(y_tmp, 1)
                for h in range(RET_HEADS):
                    dve.wait_ge(yh_done, 8 * L + h + 1)
                    V.tensor_tensor(h_lo[:, h, :], mix[:, RK + h, :], h_hi[:, h, :].bitcast(F32), ALU.subtract
                                    ).then_inc(yl_done, 1)

                def d_max(n):
                    h, b = diff_units[n]
                    s = n % 2
                    q0, nq, nk = d_cols(b)
                    dve.wait_ge(f_s, ND * L + n + 1)
                    dmask = con2("dmask")
                    if nk:
                        diag = ps[:, 3 * s:3 * s + 2, nk - P:nk]
                        V.tensor_tensor(diag, diag, dmask.unsqueeze(1).broadcast_to([P, 2, P]), ALU.add)
                    else:
                        diag = ps[0:META, 3 * s + 2, 0:2 * META].rearrange("p (a n) -> p a n", n=META)
                        V.tensor_tensor(diag, diag, dmask[0:META, 0:META].unsqueeze(1).broadcast_to([META, 2, META]),
                                        ALU.add)
                    dve.drain()
                    neg = stat[0:nq, 8 + 4 * s:10 + 4 * s]
                    V.tensor_reduce(neg, ps[0:nq, 3 * s + 2, 0:2 * META].rearrange("p (a n) -> p a n", n=META),
                                    AX.X, ALU.max)
                    if nk:
                        main = stat[:, 32 + 4 * s:34 + 4 * s]
                        V.tensor_reduce(main, ps[:, 3 * s:3 * s + 2, 0:nk], AX.X, ALU.max)
                        dve.drain()
                        V.tensor_tensor(neg, neg, main, ALU.max)
                    dve.drain()
                    V.tensor_scalar(neg, neg, -SCALE, None, ALU.mult).then_inc(f_max, 1)

                d_max(0)
                for n, (h, b) in enumerate(diff_units):
                    s = n % 2
                    q0, nq, nk = d_cols(b)
                    dve.wait_ge(f_exp, ND * L + n + 1)
                    rec = stat[0:nq, 24 + 4 * s:26 + 4 * s]
                    if nk:
                        V.tensor_tensor(rec, stat[:, 16 + 4 * s:18 + 4 * s], stat[:, 18 + 4 * s:20 + 4 * s], ALU.add)
                        dve.drain()
                        V.reciprocal(rec, rec)
                    else:
                        V.reciprocal(rec, stat[0:nq, 18 + 4 * s:20 + 4 * s])
                    dve.drain()
                    V.tensor_tensor(rec[:, 1:2], rec[:, 1:2], neg_lam[0:nq, at(L)], ALU.mult)
                    dve.drain()
                    e0, e1 = e_prob[0:nq, s, 0, 0:nk + META], e_prob[0:nq, s, 1, 0:nk + META]
                    V.tensor_scalar(e1, e1, rec[:, 1:2], None, ALU.mult)
                    dve.drain()
                    V.scalar_tensor_tensor(e0, e0, rec[:, 0:1], e1, ALU.mult, ALU.add).then_inc(f_a, 1)
                    if n + 1 < ND:
                        d_max(n + 1)
                for h in range(DIFF_HEADS):
                    dve.wait_ge(f_std, 4 * L + h + 1)
                    o = mix[:, DQ + h, :]
                    V.reciprocal(rs[:, h, :], rs[:, h, :])
                    dve.drain()
                    V.scalar_tensor_tensor(o, o, subw[:, at(L)], rs[:, h, :], ALU.mult, ALU.mult).then_inc(y_tmp, 1)
                for h in range(DIFF_HEADS):
                    dve.wait_ge(yh_done, 8 * L + 4 + h + 1)
                    V.tensor_tensor(h_lo[:, 4 + h, :], mix[:, DQ + h, :], h_hi[:, 4 + h, :].bitcast(F32), ALU.subtract
                                    ).then_inc(yl_done, 1)
                V.memset(sumsq[:, :], 0.0)
                with dve.Fori(N_MIX // 2, (N_MIX + KT) // 2) as i:
                    for s in range(2):
                        split_lo(*following(u0 + i, s))
                        dve.wait_ge(unit_done, 2 * (u0 + i) + s + 1)
                        x = tile(xT, 2 * i + s - N_MIX, T2)
                        V.tensor_tensor(halves(x, T2), halves(x, T2), bank(2 * s, T2), ALU.add).then_inc(slot_free[s], 1)
                        dve.drain()
                        add_square(x, T2)
                        dve.drain()
                dve.sem_inc(sumsq_done, 1)

            with dve.Fori(0, LAYERS) as L:
                for which in range(2):
                    stat_inverse(4 + 3 * L + 2 * which, T2)
                    h_lower(2 + 3 * L + 2 * which, 4 + 3 * L + 2 * which, T2)
                    ffn2(which, L)
                    if which == 0:
                        stat_inverse(5 + 3 * L, T2)
                        h_lower(3 + 3 * L, 5 + 3 * L, T2)
                        mixer(L)
            stat_inverse(4 + 3 * LAYERS, T2)
            for k in range(KT):
                wait(dve, y_sent[k % 2], 16 * (k // 2))
                V.scalar_tensor_tensor(tmp[:, k % 2, 0:SEQ], xT[:, k, 0:SEQ], gain[:, N_GAINS - 1, k:k + 1],
                                       rstd[:, 0:SEQ], ALU.mult, ALU.mult).then_inc(y_out, 1)

        @block.tensor
        def _(pe):
            T = nc.tensor

            def unit(half, s, out, x_hi, x_lo, ks, n, start=True, stop=True, ready=None):
                pe.wait_ge(lo_done, 2 * half + s + 1)
                for j, k in enumerate(ks):
                    if ready is not None:
                        ready(k)
                    for r, (w, x) in enumerate(((w_hi, x_hi), (w_hi, x_lo), (w_lo, x_hi))):
                        for p, c0, c1 in parts(n):
                            last = T.matmul(out[:, p, :], w[:, s, j * P:(j + 1) * P], x[:, k, c0:c1],
                                            start=start and j == 0 and r == 0,
                                            stop=stop and j == len(ks) - 1 and r == 2)
                last.then_inc(unit_done, 1)

            def sum_features(r, n):
                pe.wait_ge(sumsq_done, r + 1)
                for p, c0, c1 in parts(n):
                    last = T.matmul(bank(4, n)[:, p, :], ones, sumsq[:, c0:c1], start=True, stop=True)
                last.then_inc(stat_ps, 1)

            def carry():
                pe.sem_inc(carried, 1)

            def h_part(q):
                return lambda k: pe.wait_ge(h_lo_done, KT * q + k + 1)

            pe.wait_ge(bias_in, 32)
            for p in range(2):
                last = T.matmul(ps[0:N_BIAS, 6 + p, 0:N_DIST // 2], bias_lhs, bias_rhs[:, p * N_DIST // 2:(p + 1) * N_DIST // 2],
                                start=True, stop=True)
            last.then_inc(bias_ps, 1)
            pe.wait_ge(small_in, 16)
            sum_features(0, T1)

            def qkv_pair(i, ready=None):
                for s in range(2):
                    wait(pe, slot_free[s], i)
                    unit(i, s, bank(2 * s, T1), h_hi, h_lo, range(KT), T1, ready=ready)
            qkv_pair(0, h_part(0))
            with pe.Fori(1, N_QKV // 2) as i:
                qkv_pair(i)

            for s in range(2):
                pe.wait_ge(slot_free[s], N_QKV // 2)
            for t in range(9):
                wait(pe, vt_read, t - 3)
                for b in range(NBLK):
                    last = T.transpose(ps[:, 4 + t % 4, b * P:(b + 1) * P], qkv[:, AV + t, b * P:(b + 1) * P], ident)
                last.then_inc(vt_done, 1)
            pe.wait_ge(vt_read, 9)
            pe.wait_ge(const1_in, 16)

            def products(n):
                kind, h, b = units1[n]
                s = n % 2
                wait(pe, o_read, n - 1)
                if kind == "A":
                    lo = HD * (h % 2)
                    for g, k0, nk, _, _, tq, tk, _ in a_segments(h, b):
                        last = T.matmul(ps[:, 3 * s + g, 0:nk], qkv[lo:lo + HD, tq, rev(b)], qkv[lo:lo + HD, tk, k0:k0 + nk],
                                        start=True, stop=True)
                elif kind == "B":
                    lo, nk = HD * h, min(b + 1, 2) * P
                    for j in range(4):
                        last = T.matmul(ps[:, 3 * s + j // 2, (j % 2) * 2 * P:(j % 2) * 2 * P + nk],
                                        qkv[lo:lo + HD, BQ + j, rev(b)], qkv[lo:lo + HD, BK, (b + 1) * P - nk:(b + 1) * P],
                                        start=True, stop=True)
                else:
                    lo = HD * (h % 2)
                    for kb in range(NBLK):
                        bk, col, nq, _ = c_place(kb)
                        last = T.matmul(ps[:, 3 * s + bk, col:col + nq], qkv[lo:lo + HD, CK + h // 2, kb * P:(kb + 1) * P],
                                        qkv[lo:lo + HD, CQ + h // 2, kb * P:SEQ], start=True, stop=True)
                last.then_inc(s_done, 1)

            products(0)
            for n, (kind, h, b) in enumerate(units1):
                s = n % 2
                if n + 1 < N1:
                    products(n + 1)
                pe.wait_ge(r_done, n + 1)
                batches = t_batches(units1[n])
                for j, blocks in enumerate(batches):
                    bt = batch_at[n] + j
                    wait(pe, t_read[bt % 2], bt // 2)
                    for i, (place, _) in enumerate(blocks):
                        last = T.transpose(ps[:, 6 + bt % 2, i * P:(i + 1) * P], logit[:, s, place:place + P], ident)
                    last.then_inc(t_done, 1)
                done = batch_at[n] + len(batches)
                if kind != "C":
                    wait(pe, t_read[0], (done + 1) // 2)
                    wait(pe, t_read[1], done // 2)
                if kind == "A":
                    lo, i, n_blocks = HD * (h % 2), 0, a_width(h, b) // P
                    for g, k0, nk, _, _, _, _, tv in a_segments(h, b):
                        for kb in range(k0 // P, (k0 + nk) // P):
                            last = T.matmul(ps[lo:lo + HD, 3 * s, 0:P], qkv[:, tv, kb * P + lo:kb * P + lo + HD],
                                            probT[:, s, i, :], start=i == 0, stop=i == n_blocks - 1)
                            i += 1
                elif kind == "B":
                    lo, nb = HD * h, min(b + 1, 2)
                    for j in range(4):
                        for i in range(nb):
                            kb = b + 1 - nb + i
                            last = T.matmul(ps[lo:lo + HD, 3 * s, j * P:(j + 1) * P], qkv[:, BV, kb * P + lo:kb * P + lo + HD],
                                            probT[:, s, j * nb + i, :], start=i == 0, stop=i == nb - 1)
                else:
                    soft = probT[:, s, :, :].rearrange("p a n -> p (a n)")
                    for kb in range(NBLK):
                        bk, col, nq, place = c_place(kb)
                        last = T.matmul(ps[:, 3 * s + bk, col:col + nq], tri, soft[:, place:place + nq],
                                        start=True, stop=kb == NBLK - 1)
                        for later in range(kb + 1, NBLK):
                            _, _, nl, pl = c_place(later)
                            last = T.matmul(ps[:, 3 * s + bk, col + nq - nl:col + nq], ones, soft[:, pl:pl + nl],
                                            start=False, stop=later == NBLK - 1)
                    last.then_inc(cum_done, 1)
                    pe.wait_ge(wts_done, c_at[n] + 1)
                    lo = HD * (h % 2)
                    for kb in range(NBLK):
                        _, _, nq, place = c_place(kb)
                        last = T.matmul(ps[lo:lo + HD, 3 * s, kb * P:SEQ], qkv[:, CV + h // 2, kb * P + lo:kb * P + lo + HD],
                                        logit[:, s, place:place + nq], start=kb == 0, stop=kb == NBLK - 1)
                last.then_inc(o_done, 1)

            pe.wait_ge(o_read, N1)
            pe.wait_ge(ol_done, 2)
            with pe.Fori(0, KT // 2) as i:
                for odd in range(2):
                    half = U_MERGE // 2 + 4 * i + 2 * odd
                    for n in range(3):
                        s = (odd + n) % 2
                        pe.wait_ge(slot_free[s], G_GATE // 2 + 3 * i + (3 * odd + n) // 2)
                        unit(half + n // 2, n % 2, bank(2 * s, T1), h_hi, h_lo, range(KT), T1)
                    pe.wait_ge(br_free, 2 * i + odd + 1)
                    pe.wait_ge(lo_done, 2 * half + 4)
                    for br, ks in enumerate((range(0, 2), range(2, 6), range(6, 8))):
                        for k in ks:
                            for r, (w, x) in enumerate(((w_hi, o_hi), (w_hi, o_lo), (w_lo, o_hi))):
                                last = T.matmul(ps[:, 4 + br, :], w[:, 1, k * P:(k + 1) * P], x[:, k, :],
                                                start=k == ks[0] and r == 0, stop=k == ks[-1] and r == 2)
                    last.then_inc(unit_done, 1)

            def out_pair(i):
                for s in range(2):
                    pe.wait_ge(slot_free[s], G_OUT1 // 2 + i)
                    unit(U_OUT1 // 2 + i, s, bank(2 * s, T1), m_hi, m_lo, range(KT), T1)
            pe.wait_ge(ml_done, KT)
            with pe.Fori(0, KT // 2) as i:
                out_pair(i)
            sum_features(1, T1)
            sum_features(2, T1)

            for part in range(2):
                half0 = (U_FF1 + UNITS_FF1_HALF * part) // 2
                slot0 = (G_FF1 + GROUPS_FF1_HALF * part) // 2

                def up_pair(j, ready=None):
                    for s in range(2):
                        pe.wait_ge(slot_free[s], slot0 + j)
                        unit(half0 + j, s, bank(2 * s, T1), h_hi, h_lo, range(KT), T1, ready=ready)
                if part == 0:
                    up_pair(0, h_part(1))
                with pe.Fori(1 - part, FF1_HALF) as j:
                    up_pair(j)
                with pe.Fori(0, KT // 2) as i:
                    for s in range(2):
                        pe.wait_ge(slot_free[s], slot0 + FF1_HALF + i)
                        for n in range(2):
                            pe.wait_ge(al_done, FF1_HALF * part + KT * (n + 1))
                            unit(half0 + FF1_HALF + 2 * i + s, n, bank(2 * s, T1), f1_hi, f1_lo,
                                 range(KT * n, KT * (n + 1)), T1, start=n == 0, stop=n == 1)
            sum_features(3, T1)

            def ffn2(which, L):
                u0, g0, a0 = ffn2_base(which, L)

                def up_pair(j, ready=None):
                    for s in range(2):
                        pe.wait_ge(slot_free[s], g0 + j)
                        unit(u0 + j, s, bank(2 * s, T2), h_hi, h_lo, range(KT), T2, ready=ready)
                up_pair(0, h_part(2 + 3 * L + 2 * which))
                with pe.Fori(1, FF2_TILES) as j:
                    up_pair(j)
                with pe.Fori(0, KT // 2) as i:
                    for s in range(2):
                        pe.wait_ge(slot_free[s], g0 + FF2_TILES + i)
                        for n in range(3):
                            c, ks = 3 * s + n, range(KT * n, min(KT * (n + 1), FF2_TILES))
                            pe.wait_ge(al_done, a0 + ks[-1] + 1)
                            unit(u0 + FF2_TILES + 3 * i + c // 2, c % 2, bank(2 * s, T2), f2_hi, f2_lo, ks, T2,
                                 start=n == 0, stop=n == 2)

            def mixer(L):
                u0, g0 = mix_base(L)

                def pair(i, x_ready=None):
                    for s in range(2):
                        pe.wait_ge(slot_free[s], g0 + i)
                        unit(u0 + i, s, bank(2 * s, T2), h_hi, h_lo, range(KT), T2, ready=x_ready)
                pair(0, h_part(3 + 3 * L))
                with pe.Fori(1, N_MIX // 2) as i:
                    pair(i)
                for s in range(2):
                    pe.wait_ge(slot_free[s], g0 + N_MIX // 2)
                for t, tl in enumerate(tp_tiles):
                    if t >= 2:
                        pe.wait_ge(tp_dve, NTP * L + t - 1)
                        pe.wait_ge(tp_act, 8 * L + min(t - 1, 8))
                    for b in range(NBLK if t < 8 else NBLK - 1):
                        T.transpose(ps[:, 4 + t % 2, b * P:(b + 1) * P], mix[:, tl, b * P:(b + 1) * P], ident)
                    T.transpose(ps[0:META, 6 + t % 2, 0:P], mix[:, tl, SEQ:T2], ident).then_inc(tp_done, 1)
                pe.wait_ge(tp_dve, NTP * (L + 1))
                for h in range(RET_HEADS):
                    for b in range(NBLK):
                        c = slice(b * P, (b + 1) * P)
                        T.matmul(ps[:, h, c], mix[:, RK + h, c], mix[:, RQ + h, c], start=True, stop=True)
                    T.matmul(ps[0:META, 4 + h, 0:META], mix[:, RK + h, SEQ:T2], mix[:, RQ + h, SEQ:T2],
                             start=True, stop=True).then_inc(sc_done, 1)
                for h in range(RET_HEADS):
                    pe.wait_ge(sd_done, 4 * L + h + 1)
                    T.matmul(ps[:, h, 0:P], kd_meta[:, h, :], v_meta[:, h, :], start=True, stop=True)
                    for b in range(NBLK - 1):
                        last = T.matmul(ps[:, h, (b + 1) * P:(b + 2) * P], kd[:, h, b, :], mix[:, RV + h, b * P:(b + 1) * P],
                                        start=True, stop=True)
                    last.then_inc(st_done, 1)
                pe.wait_ge(state_done, L + 1)
                for h in range(RET_HEADS):
                    for b in range(NBLK):
                        c = slice(b * P, (b + 1) * P)
                        T.matmul(ps[:, 4 + h, c], mix[:, RV + h, c], sd[:, h, c], start=True, stop=False)
                        T.matmul(ps[:, 4 + h, c], state[:, h, b, :], mix[:, RQ + h, c], start=False, stop=True)
                    T.matmul(ps[:, h, 0:META], v_meta[:, h, :], sd_meta[:, h, :], start=True, stop=True
                             ).then_inc(ro_done, 1)
                pe.wait_ge(ro_read, 4 * (L + 1))
                for h in range(RET_HEADS):
                    for p, c0, c1 in parts(T2):
                        last = T.matmul(bank(2 * h, T2)[:, p, :], ones, mix[:, RK + h, c0:c1], start=True, stop=True)
                    last.then_inc(mu_done, 1)
                for h in range(RET_HEADS):
                    pe.wait_ge(sq_done, 4 * L + h + 1)
                    for p, c0, c1 in parts(T2):
                        last = T.matmul(bank(2 * h, T2)[:, p, :], ones, tmp[:, h, c0:c1], start=True, stop=True)
                    last.then_inc(var_done, 1)

                def d_products(n):
                    h, b = diff_units[n]
                    s = n % 2
                    q0, nq, nk = d_cols(b)
                    if n >= 2:
                        pe.wait_ge(f_o_read, ND * L + n - 1)
                        if not nk:
                            carry()

                    def map_products(m, key0, key1, out):
                        rows = slice(HD * m, HD * (m + 1))
                        return T.matmul(out, mix[rows, DQ + h, q0:q0 + nq], mix[rows, DK + h, key0:key1],
                                        start=True, stop=True)
                    map_products(0, SEQ, T2, ps[0:nq, 3 * s + 2, 0:META]).then_inc(m0_done, 1)
                    if nk:
                        for m in range(2):
                            map_products(m, 0, nk, ps[0:nq, 3 * s + m, 0:nk])
                    pe.wait_ge(m0_done, ND * L + n + 1)
                    if not nk:
                        carry()
                    map_products(1, SEQ, T2, ps[0:nq, 3 * s + 2, META:2 * META]).then_inc(f_s, 1)

                pe.wait_ge(vstd_done, 4 * (L + 1))
                carry()
                d_products(0)
                full = 0
                for n, (h, b) in enumerate(diff_units):
                    s = n % 2
                    q0, nq, nk = d_cols(b)
                    if n + 1 < ND:
                        d_products(n + 1)
                    pe.wait_ge(f_a, ND * L + n + 1)
                    if n:
                        pe.wait_ge(f_read_meta, ND * L + n)
                    if full:
                        pe.wait_ge(f_read, (ND - DIFF_HEADS) * L + full)
                    if not nk:
                        carry()
                    for b2 in range(nk // P):
                        T.transpose(ps[:, 6, b2 * P:(b2 + 1) * P], e_prob[:, s, 0, b2 * P:(b2 + 1) * P], ident)
                    T.transpose(ps[0:META, 7, 0:nq], e_prob[0:nq, s, 0, nk:nk + META], ident[0:nq, 0:nq]).then_inc(f_t, 1)
                    full += nk > 0
                    if nk:
                        pe.wait_ge(f_read, (ND - DIFF_HEADS) * L + full)
                    for b2 in range(nk // P):
                        T.matmul(ps[:, 3 * s, 0:nq], mix[:, DV + h, b2 * P:(b2 + 1) * P], aT[:, s, b2 * P:(b2 + 1) * P],
                                 start=b2 == 0, stop=False)
                    pe.wait_ge(f_read_meta, ND * L + n + 1)
                    T.matmul(ps[:, 3 * s, 0:nq], v_meta[:, 4 + h, :], aT_meta[:, s, 0:nq], start=nk == 0, stop=True
                             ).then_inc(f_o, 1)
                for h in range(DIFF_HEADS):
                    pe.wait_ge(f_sq, 4 * L + h + 1)
                    for p, c0, c1 in parts(T2):
                        last = T.matmul(bank(2 * h, T2)[:, p, :], ones, tmp[:, h, c0:c1], start=True, stop=True)
                    last.then_inc(f_sum, 1)
                pe.wait_ge(f_std, 4 * (L + 1))
                pe.wait_ge(yl_done, 8 * (L + 1))
                carry()
                with pe.Fori(N_MIX // 2, (N_MIX + KT) // 2) as i:
                    pair(i)

            with pe.Fori(0, LAYERS) as L:
                for which in range(2):
                    sum_features(4 + 3 * L + 2 * which, T2)
                    ffn2(which, L)
                    if which == 0:
                        sum_features(5 + 3 * L, T2)
                        mixer(L)
            sum_features(4 + 3 * LAYERS, T2)


def bucket(dist):
    exact = N_BUCKETS // 2
    nf = np.maximum(dist, 1).astype(np.float32)
    large = exact + (np.log(nf / np.float32(exact)) / np.float32(math.log(2048 / exact))
                     * np.float32(N_BUCKETS - exact)).astype(np.int32)
    return np.where(dist < exact, dist, np.minimum(large, N_BUCKETS - 1))


def bias_table():
    dist = SEQ - 1 - np.arange(N_DIST)
    rows = np.zeros((BIAS_ROWS, N_DIST), np.float32)
    rows[bucket(np.maximum(dist, 0)), np.arange(N_DIST)] = 1.0
    allowed = [(dist >= 0) & (dist <= 128), (dist >= 0) & (dist % 4 == 0), (dist >= 0) & (dist % 16 == 0),
               (dist >= 0) & (dist <= 127)]
    for r, ok in enumerate(allowed):
        rows[N_BUCKETS + r] = np.where(ok, 0.0, NEG)
    return rows


def constants2():
    out = np.zeros((P, N_CONST2), np.float32)

    def put(name, a):
        c, n = CONST2[name]
        out[:a.shape[0], c:c + n] = a.reshape(a.shape[0], n)

    f = np.float32
    pos = np.concatenate([np.arange(META, T2), np.arange(META)]).astype(f)
    angle = np.power(f(10000.0), -np.linspace(0.0, 1.0, P // 2, dtype=f)).astype(f)
    freq = (angle[:, None] * pos[None, :]).astype(f)
    put("cos_r", np.concatenate([np.cos(freq)] * 2))
    put("sin_r", np.concatenate([-np.sin(freq), np.sin(freq)]))
    inv = np.power(f(500000.0), -np.arange(0, 16, 2, dtype=f) / f(16)).astype(f)
    freq = (inv[:, None] * pos[None, :]).astype(f)
    cos, sin = np.ones((P, T2), f), np.zeros((P, T2), f)
    for m in range(2):
        for part, sign in ((0, -1), (1, 1)):
            rows = slice(HD * m + 32 * part, HD * m + 32 * part + 8)
            cos[rows], sin[rows] = np.cos(freq), sign * np.sin(freq)
    put("cos_d", cos)
    put("sin_d", sin)
    gamma = np.log(1.0 - 2.0 ** (-5.0 - np.arange(RET_HEADS)))
    i = np.arange(P)
    rel = i[None, :] - i[:, None]
    scale = P ** -0.5
    put("decay", np.stack([np.where(rel >= 0, np.exp(g * np.maximum(rel, 0)), 0.0) * scale for g in gamma], 1))
    put("q_decay", np.broadcast_to(np.exp(gamma[:, None] * (i + 1)), (P, RET_HEADS, P)))
    kd = np.exp(gamma[None, :] * (P - 1 - i)[:, None]) * scale
    put("k_decay", kd)
    put("k_decay_meta", kd[P - META:])
    put("dmask", np.where(i[None, :] > i[:, None], NEG, 0.0))
    return out


def kernel(**inp):
    import concourse.bacc as bacc
    from concourse.bass_utils import run_bass_kernel_spmd

    a = {k: np.asarray(v) for k, v in inp.items()}

    def tiles(w, cols, rows=None):
        w = w[:, cols]
        if rows is not None:
            w = w[rows]
        return w.reshape(w.shape[0] // P, P, w.shape[1] // P, P).transpose(0, 2, 1, 3)

    def units(t):
        return t.transpose(0, 2, 1, 3).reshape(t.shape[0], P, KT * P)

    w_in = a["w_in"][0]
    off_bq, off_bkv = 2304, 2304 + 512
    off_c, off_gate = off_bkv + 256, off_bkv + 256 + 768
    b_perm = np.concatenate([np.arange(HD) + HD * (i + 4 * g) for i in range(4) for g in range(2)])
    cols = np.concatenate([np.arange(1536), off_bq + b_perm, off_bkv + np.arange(128), off_c + np.arange(512),
                           1536 + np.arange(768), off_bkv + 128 + np.arange(128), off_c + 512 + np.arange(256)])
    stream = [units(tiles(w_in, cols).transpose(1, 0, 2, 3))]
    gate = tiles(w_in, off_gate + np.arange(3 * DM)).transpose(1, 0, 2, 3).reshape(3, KT, KT, P, P)
    branch = np.concatenate([a["w_br_a"][0], a["w_br_b"][0][b_perm], a["w_br_c"][0]])
    branch = tiles(branch, np.arange(DM)).transpose(1, 0, 2, 3)
    merge = np.concatenate([gate.transpose(1, 0, 2, 3, 4), branch[:, None]], 1).reshape(4 * KT, KT, P, P)
    stream.append(units(merge))
    stream.append(units(tiles(a["w_out"][0], np.arange(DM)).transpose(1, 0, 2, 3)))
    up = tiles(a["w_up"][0], np.arange(2 * FF1_TILES * P)).transpose(1, 0, 2, 3)
    up = up.reshape(2, FF1_TILES, KT, P, P).transpose(1, 0, 2, 3, 4)
    down = tiles(a["w_down"][0], np.arange(DM))
    for part in range(2):
        j = slice(FF1_HALF * part, FF1_HALF * (part + 1))
        stream.append(units(up[j].reshape(2 * FF1_HALF, KT, P, P)))
        stream.append(units(down[j].transpose(1, 0, 2, 3).reshape(2 * KT, KT, P, P)))

    ret = np.concatenate([P * h + np.concatenate([np.arange(0, P, 2), np.arange(1, P, 2)]) for h in range(4)])
    head = np.concatenate([np.arange(8), 16 + np.arange(24), 8 + np.arange(8), 40 + np.arange(24)])
    att = np.concatenate([HD * h + head for h in range(8)])
    plain = np.arange(512)
    mix_cols = np.concatenate([ret, 512 + ret, 2048 + att, 2560 + att, 1024 + plain, 3072 + plain, 1536 + plain])
    for l in range(LAYERS):
        for f in ("ffn1", "ffn2"):
            pair = np.stack([tiles(a[f"{f}_{w}_2"][l], np.arange(FF2_TILES * P)).transpose(1, 0, 2, 3)
                             for w in ("w_gate", "w_up")], 1)
            stream.append(units(pair.reshape(2 * FF2_TILES, KT, P, P)))
            d = tiles(a[f"{f}_w_down_2"][l], np.arange(DM)).transpose(1, 0, 2, 3)
            d = np.concatenate([d, np.zeros((KT, 3 * KT - FF2_TILES, P, P), d.dtype)], 1)
            stream.append(units(d.reshape(3 * KT, KT, P, P)))
            if f == "ffn1":
                stream.append(units(tiles(a["w_in_2"][l], mix_cols).transpose(1, 0, 2, 3)))
                stream.append(units(tiles(a["w_out_2"][l], np.arange(DM)).transpose(1, 0, 2, 3)))
    stream.append(np.zeros((N_STREAM - N_UNITS, P, KT * P), np.float32))
    stream = np.concatenate(stream)
    assert stream.shape[0] == N_STREAM

    params = np.zeros((P, N_PARAMS), np.float32)

    def put(name, v):
        c, n = PARAMS[name]
        params[:, c:c + n] = v.reshape(v.shape[0], n) if v.ndim > 1 else v

    gains = [a["attn_pre_norm"][0], a["attn_post_norm"][0], a["ffn_pre_norm"][0], a["ffn_post_norm"][0]]
    for l in range(LAYERS):
        gains += [a["ffn1_norm_2"][l], a["mix_norm_2"][l], a["ffn2_norm_2"][l]]
    gains.append(a["final_norm_2"])
    put("gain", np.stack(gains).reshape(N_GAINS, KT, P).transpose(2, 0, 1))
    put("b_gate", a["b_gate"][0].reshape(3, KT, P).transpose(2, 0, 1))
    taps = np.concatenate([a["conv_w"][0], a["conv_b"]])
    put("conv", taps.reshape(4, 2 * FF1_TILES, P).transpose(2, 1, 0))
    put("sinks", np.broadcast_to(a["sinks"][0], (P, B_HEADS)))
    put("gn", a["ret_gn_w_2"].reshape(LAYERS, 4, P).transpose(2, 0, 1))
    put("subln", a["diff_subln_w_2"].T)
    lams = np.stack([a[f"diff_lambda_{n}_2"] for n in ("q1", "k1", "q2", "k2")], 1)
    put("lams", np.broadcast_to(lams, (P, LAYERS, 4, HD)))
    put("ident", np.eye(P, dtype=np.float32))
    put("ones", np.ones((P, P), np.float32))
    put("eps", np.full((P, 1), EPS, np.float32))
    init = np.array([0.8 - 0.6 * math.exp(-0.3 * l) for l in range(LAYERS)])
    put("lam_init", np.broadcast_to(init, (P, LAYERS)))
    put("one_minus_init", np.broadcast_to(1.0 - init, (P, LAYERS)))

    const1 = np.zeros((P, N_CONST1), np.float32)
    i = np.arange(P)
    const1[:, 0:P] = i[:, None] >= i[None, :]
    const1[:, P:2 * P] = np.where(i[:, None] >= i[None, :], NEG, 0.0)
    bias_lhs = np.zeros((BIAS_ROWS, N_BIAS), np.float32)
    bias_lhs[:N_BUCKETS] = a["rel_bias"]
    for g in range(3):
        bias_lhs[N_BUCKETS + g, A_HEADS * g:A_HEADS * (g + 1)] = 1.0
    bias_lhs[N_BUCKETS + 3, 3 * A_HEADS:] = 1.0

    def by_feature(x):
        return x.reshape(x.shape[0], KT, P).transpose(2, 1, 0)

    arrays = {
        "x": by_feature(a["x"][0]), "meta": by_feature(a["meta_tokens_2"]), "stream": stream, "params": params,
        "const1": const1, "const2": constants2(), "bias_lhs": bias_lhs, "bias_rhs": bias_table(),
    }
    arrays = {k: np.ascontiguousarray(v, dtype=np.float32) for k, v in arrays.items()}
    nc = bacc.Bacc("TRN2", target_bir_lowering=False, num_devices=1)
    d = {k: nc.dram_tensor("in_" + k, v.shape, F32, kind="ExternalInput").ap() for k, v in arrays.items()}
    out = nc.dram_tensor("out", [KT, P, SEQ], F32, kind="ExternalOutput").ap()
    scratch = nc.dram_tensor("bias_scratch", [N_BIAS, N_DIST], F32).ap()
    program(nc, d["x"], d["meta"], d["stream"], d["params"], d["const1"], d["const2"], d["bias_lhs"], d["bias_rhs"],
            scratch, out)
    r = run_bass_kernel_spmd(nc, [{"in_" + k: v for k, v in arrays.items()}], core_ids=[0])
    y = r.results[0]["out"]
    return np.ascontiguousarray(y.transpose(2, 0, 1).reshape(1, SEQ, DM))
```
